# Optimizing a Trainium2 kernel written in Bass

```python
import jax, jax.numpy as jnp
from jax import lax
import numpy as np

D_MODEL = 1024
BATCH = 1
SEQ = 512
DEPTH = 1

D_MIX = D_MODEL
D_ATTN = D_MIX // 2
N_ATTN_HEADS = 8
HEAD_DIM = D_ATTN // N_ATTN_HEADS
D_CONV = D_MIX - D_ATTN
CONV_WIDTH = 31
Q_BLOCK = 128
D_IN_PROJ = 3 * D_ATTN + N_ATTN_HEADS + 2 * D_CONV
N_KEYS = 128
N_EXPERTS = N_KEYS * N_KEYS
PEER_HEADS = 8
PEER_QUERY_DIM = 256
PEER_HALF = PEER_QUERY_DIM // 2
PEER_TOPK = 16
PEER_CHUNK = 128
D_PLE = 256
EPS = 1e-6
LN_EPS = 1e-5

kernel_name = "hymba_fox_conformer_peer_layer"

def rmsnorm(x, g, eps=EPS):
    xf = x.astype(jnp.float32)
    y = xf * lax.rsqrt(jnp.mean(xf * xf, axis=-1, keepdims=True) + eps)
    return (y * g.astype(jnp.float32)).astype(x.dtype)

def layernorm(x, g, b, eps=LN_EPS):
    xf = x.astype(jnp.float32)
    mu = jnp.mean(xf, axis=-1, keepdims=True)
    var = jnp.mean(jnp.square(xf - mu), axis=-1, keepdims=True)
    y = (xf - mu) * lax.rsqrt(var + eps)
    return (y * g.astype(jnp.float32) + b.astype(jnp.float32)).astype(x.dtype)

def forgetting_attention(q, k, v, logf):
    b, s, h, dh = q.shape
    scale = dh ** -0.5
    qh = q.transpose(0, 2, 1, 3)
    kh = k.transpose(0, 2, 1, 3)
    vh = v.transpose(0, 2, 1, 3)
    F = jnp.cumsum(logf.astype(jnp.float32), axis=1).transpose(0, 2, 1)
    outs = []
    for blk in range(s // Q_BLOCK):
        q0 = blk * Q_BLOCK
        end = q0 + Q_BLOCK
        qb = qh[:, :, q0:end]
        kb = kh[:, :, :end]
        vb = vh[:, :, :end]
        logits = jnp.einsum('bhqd,bhkd->bhqk', qb, kb).astype(jnp.float32) * scale
        logits = logits + F[:, :, q0:end, None] - F[:, :, None, :end]
        qpos = q0 + jnp.arange(Q_BLOCK)
        kpos = jnp.arange(end)
        mask = qpos[:, None] >= kpos[None, :]
        logits = jnp.where(mask[None, None], logits, jnp.finfo(jnp.float32).min)
        probs = jax.nn.softmax(logits, axis=-1)
        outs.append(jnp.einsum('bhqk,bhkd->bhqd', probs.astype(vb.dtype), vb))
    o = jnp.concatenate(outs, axis=2)
    return o.transpose(0, 2, 1, 3).reshape(b, s, h * dh)

def conformer_conv(a, g, conv_w, conv_b, ln_g, ln_b):
    u = a * jax.nn.sigmoid(g)
    y = lax.conv_general_dilated(
        u, conv_w.astype(u.dtype), window_strides=(1,), padding=[(CONV_WIDTH - 1, 0)],
        dimension_numbers=('NWC', 'WIO', 'NWC'), feature_group_count=D_CONV)
    y = y + conv_b.astype(y.dtype)
    y = layernorm(y, ln_g, ln_b)
    return jax.nn.silu(y)

def peer_ffn(xn, w_q, sub_keys1, sub_keys2, expert_u, expert_v):
    b, s, d = xn.shape
    qp = (xn @ w_q).reshape(b, s, PEER_HEADS, PEER_QUERY_DIM)
    q1, q2 = qp[..., :PEER_HALF], qp[..., PEER_HALF:]
    s1 = jnp.einsum('bshd,kd->bshk', q1, sub_keys1).astype(jnp.float32)
    s2 = jnp.einsum('bshd,kd->bshk', q2, sub_keys2).astype(jnp.float32)
    v1, i1 = lax.top_k(s1, PEER_TOPK)
    v2, i2 = lax.top_k(s2, PEER_TOPK)
    cand = (v1[..., :, None] + v2[..., None, :]).reshape(b, s, PEER_HEADS, PEER_TOPK * PEER_TOPK)
    vs, ic = lax.top_k(cand, PEER_TOPK)
    e1 = jnp.take_along_axis(i1, ic // PEER_TOPK, axis=-1)
    e2 = jnp.take_along_axis(i2, ic % PEER_TOPK, axis=-1)
    idx = e1 * N_KEYS + e2
    gates = jax.nn.softmax(vs, axis=-1)
    t = b * s
    n_sel = PEER_HEADS * PEER_TOPK
    xt = xn.reshape(t // PEER_CHUNK, PEER_CHUNK, d)
    it = idx.reshape(t // PEER_CHUNK, PEER_CHUNK, n_sel)
    gt = gates.reshape(t // PEER_CHUNK, PEER_CHUNK, n_sel).astype(xn.dtype)

    def chunk_fn(args):
        xc, ic_, gc = args
        act = jax.nn.gelu(jnp.einsum('ckd,cd->ck', expert_u[ic_], xc))
        return jnp.einsum('ck,ckd->cd', gc * act, expert_v[ic_])

    out = lax.map(chunk_fn, (xt, it, gt))
    return out.reshape(b, s, d)

def setup_inputs(seed: int = 0) -> dict:
    key = jax.random.key(seed)
    ks = jax.random.split(key, 24)
    f32 = jnp.float32
    nrm = lambda k, shape, sc: jax.random.normal(k, shape, f32) * sc
    gain = lambda k, shape: 1.0 + 0.05 * jax.random.normal(k, shape, f32)
    L = DEPTH
    return {
        "x": nrm(ks[0], (BATCH, SEQ, D_MODEL), 1.0),
        "p": nrm(ks[1], (DEPTH, BATCH, SEQ, D_PLE), 1.0),
        "ln_mix": gain(ks[2], (L, D_MODEL)),
        "w_in": nrm(ks[3], (L, D_MODEL, D_IN_PROJ), D_MODEL ** -0.5),
        "b_fgate": 2.0 + 0.5 * jax.random.normal(ks[4], (L, N_ATTN_HEADS), f32),
        "q_norm": gain(ks[5], (L, HEAD_DIM)),
        "k_norm": gain(ks[6], (L, HEAD_DIM)),
        "conv_w": nrm(ks[7], (L, CONV_WIDTH, 1, D_CONV), CONV_WIDTH ** -0.5),
        "conv_b": nrm(ks[8], (L, D_CONV), 0.02),
        "conv_ln_g": gain(ks[9], (L, D_CONV)),
        "conv_ln_b": nrm(ks[10], (L, D_CONV), 0.02),
        "attn_out_norm": gain(ks[11], (L, D_ATTN)),
        "conv_out_norm": gain(ks[12], (L, D_CONV)),
        "w_out": nrm(ks[13], (L, D_MIX, D_MODEL), D_MIX ** -0.5),
        "ln_ffn": gain(ks[14], (L, D_MODEL)),
        "w_peer_q": nrm(ks[15], (L, D_MODEL, PEER_HEADS * PEER_QUERY_DIM), D_MODEL ** -0.5),
        "sub_keys1": nrm(ks[16], (L, N_KEYS, PEER_HALF), PEER_HALF ** -0.5),
        "sub_keys2": nrm(ks[17], (L, N_KEYS, PEER_HALF), PEER_HALF ** -0.5),
        "expert_u": nrm(ks[18], (L, N_EXPERTS, D_MODEL), D_MODEL ** -0.5),
        "expert_v": nrm(ks[19], (L, N_EXPERTS, D_MODEL), PEER_HEADS ** -0.5),
        "ln_pl": gain(ks[20], (L, D_MODEL)),
        "w_pl_gate": nrm(ks[21], (L, D_MODEL, D_MODEL), D_MODEL ** -0.5),
        "w_pl_proj": nrm(ks[22], (L, D_PLE, D_MODEL), D_PLE ** -0.5),
    }

def reference(x, p, ln_mix, w_in, b_fgate, q_norm, k_norm, conv_w, conv_b, conv_ln_g, conv_ln_b,
              attn_out_norm, conv_out_norm, w_out, ln_ffn, w_peer_q, sub_keys1, sub_keys2,
              expert_u, expert_v, ln_pl, w_pl_gate, w_pl_proj):
    b, s, _ = x.shape
    h = x
    for i in range(DEPTH):
        xn = rmsnorm(h, ln_mix[i])
        z = xn @ w_in[i]
        o = 0
        q = z[..., o:o + D_ATTN]; o += D_ATTN
        k = z[..., o:o + D_ATTN]; o += D_ATTN
        v = z[..., o:o + D_ATTN]; o += D_ATTN
        f_logit = z[..., o:o + N_ATTN_HEADS]; o += N_ATTN_HEADS
        glu_a = z[..., o:o + D_CONV]; o += D_CONV
        glu_g = z[..., o:o + D_CONV]
        q = rmsnorm(q.reshape(b, s, N_ATTN_HEADS, HEAD_DIM), q_norm[i])
        k = rmsnorm(k.reshape(b, s, N_ATTN_HEADS, HEAD_DIM), k_norm[i])
        v = v.reshape(b, s, N_ATTN_HEADS, HEAD_DIM)
        logf = jax.nn.log_sigmoid(f_logit.astype(jnp.float32) + b_fgate[i].astype(jnp.float32))
        y_attn = forgetting_attention(q, k, v, logf)
        y_conv = conformer_conv(glu_a, glu_g, conv_w[i], conv_b[i], conv_ln_g[i], conv_ln_b[i])
        y = jnp.concatenate([rmsnorm(y_attn, attn_out_norm[i]),
                             rmsnorm(y_conv, conv_out_norm[i])], axis=-1)
        h = h + y @ w_out[i]
        h = h + peer_ffn(rmsnorm(h, ln_ffn[i]), w_peer_q[i], sub_keys1[i], sub_keys2[i],
                         expert_u[i], expert_v[i])
        gate = jax.nn.sigmoid(rmsnorm(h, ln_pl[i]) @ w_pl_gate[i])
        h = h + gate * (p[i] @ w_pl_proj[i])
    return h


_drawn_inputs = setup_inputs


def setup_inputs(seed=0):
    import zlib

    import numpy as np

    out = dict(_drawn_inputs(seed))
    spreads = {}
    factors = {'conv_ln_b': 3.472, 'ln_pl': 8.0}
    for name, (base, spread) in spreads.items():
        noise = np.random.default_rng([zlib.crc32(name.encode()), seed]).standard_normal(out[name].shape)
        drawn = base * np.exp(spread * noise) if base else spread * noise
        out[name] = __import__('jax').numpy.asarray(drawn.astype(out[name].dtype))
    for name, factor in factors.items():
        out[name] = (out[name] * factor).astype(out[name].dtype)
    return out
```

```python
from contextlib import ExitStack

import concourse.bass as bass
from concourse import mybir
from concourse.alu_op_type import AluOpType as ALU

F32, F32R, BF16, U32 = mybir.dt.float32, mybir.dt.float32r, mybir.dt.bfloat16, mybir.dt.uint32
ACT = mybir.ActivationFunctionType
AX = mybir.AxisListType

P = 128
D = 1024
S = 512
TT = S // P
KC = D // P
DA = 512
CC = DA // P
H = 8
DH = DA // H
CW = 31
PH = 8
TOP = 16
NK = 128
PLE = 256
EPS, LN_EPS = 1e-6, 1e-5
NEG = -1e38

PROJ = 0
GLU = PROJ + PLE // P
FG = GLU + 2 * CC
QK = FG + 1
VV = QK + 2 * CC
WO = VV + CC
PQ = WO + KC
EU = PQ + 2 * PH
EV = EU + NK
GA = EV + NK
END = GA + KC
RING = 4
LEAD = 3
STEP = 16
CLEAD = 2
CHUNK = 32
GT = 4
GW = GT * CHUNK
UT = 4
UNITS = P // UT
UCHUNK = CHUNK // UT
URING = 4

C_LNMIX, C_LNFFN, C_LNPL, C_YG = 0, KC, 2 * KC, 3 * KC
C_QN = 4 * KC
C_KN = C_QN + 1
C_BF = C_KN + 1
C_CB = C_BF + 1
C_CW = C_CB + CC
C_END = C_CW + CC * CW
N_CONSTS = 26


def slot(s):
    return s % RING


def hybrid_layer(nc, x, pT, stream, cols, rows, keysT, out, act_dram, gate_dram):
    ctx = ExitStack()
    with ctx:
        def sb(name, shape, dt=F32):
            return ctx.enter_context(nc.sbuf_tensor(name, shape, dt))

        def sem(name):
            return ctx.enter_context(nc.semaphore(name))

        xs = sb("xs", [P, TT, D])
        pp = sb("pp", [P, TT, D])
        raw = sb("raw", [P, RING, D])
        whi = sb("whi", [P, RING, D], F32R)
        wlo = sb("wlo", [P, RING, D], F32R)
        ahi = sb("ahi", [P, KC, S], F32R)
        alo = sb("alo", [P, KC, S], F32R)
        colc = sb("colc", [P, C_END])
        ident = sb("ident", [P, P])
        iota = sb("iota", [P, P])
        epsc = sb("epsc", [P, 2])
        qgain = sb("qgain", [P, 1])
        ss = sb("ss", [P, 4, TT, 2])
        ms = sb("ms", [P, 4, TT, 2])
        sd = sb("sd", [P, 4, TT, 2])
        rs = sb("rs", [P, 4, TT, 2])
        diag = sb("diag", [P, TT, 2, P])
        xf = sb("xf", [P, 2, S])
        junk = sb("junk", [P, D])
        ps = ctx.enter_context(nc.psum_tensor("ps", [P, 8, S], F32))

        front = ctx.enter_context(ExitStack())

        def fb(name, shape, dt=F32):
            return front.enter_context(nc.sbuf_tensor(name, shape, dt))

        lnrows = fb("lnrows", [P, 2, DA])
        negmask = fb("negmask", [P, P], BF16)
        identb = fb("identb", [P, P], BF16)
        blk = fb("blk", [P, 2 * CC, 2 * H])
        self_ = fb("self_", [P, H, P], BF16)
        selq = fb("selq", [P, 2 * CC, P], BF16)
        glu_flat = fb("glu_flat", [P, CC * (CW - 1 + S)])
        glu = glu_flat[:].rearrange("p (c n) -> p c n", c=CC)
        yc = glu_flat[:, 0:TT * DA].rearrange("p (t n) -> p t n", t=TT)
        cy = fb("cy", [P, CC, S])
        vt = fb("vt", [P, TT, DA + DH])
        f3 = fb("f3", [P, S], BF16)
        r3 = fb("r3", [P, S], BF16)
        nmax = fb("nmax", [P, TT * H])
        den = fb("den", [P, TT * H])
        rden = fb("rden", [P, TT * H])
        bn = fb("bn", [P, TT, 6])
        mv = fb("mv", [P, TT, 2])
        lsd = fb("lsd", [P, TT])
        lrs = fb("lrs", [P, TT])
        with ExitStack() as only_projection:
            def ob(name, shape, dt=F32):
                return only_projection.enter_context(nc.sbuf_tensor(name, shape, dt))

            p_raw = ob("p_raw", [P, PLE // P, S])
            p_hi = ob("p_hi", [P, PLE // P, S], F32R)
            p_lo = ob("p_lo", [P, PLE // P, S], F32R)
        qk = fb("qk", [P, 2 * CC, S])
        with ExitStack() as before_attention:
            def ob(name, shape, dt=F32):
                return before_attention.enter_context(nc.sbuf_tensor(name, shape, dt))

            sig = ob("sig", [P, 2, S])
            sq = ob("sq", [P, 2, S])
            rt = ob("rt", [2 * H, S])
            rr = ob("rr", [2 * H, 2, S])
            fz = ob("fz", [H, 4, S])
            negf = ob("negf", [H, 2, S])
            mid = ob("mid", [2 * H, S], BF16)
        vT = sig
        pr = fb("pr", [P, 3, S])
        pT_sb = fb("pT_sb", [P, 2, S])
        att = fb("att", [P, TT, DA])
        csg = fb("csg", [P, 2, DA])
        front.close()

        peer = ctx.enter_context(ExitStack())

        def eb(name, shape, dt=F32):
            return peer.enter_context(nc.sbuf_tensor(name, shape, dt))

        kT = eb("kT", [P, 2, NK])
        qp = eb("qp", [P, 2, S])
        hout = eb("hout", [P, RING, S])
        egb = eb("egb", [P, TT, 3, P])
        egs = eb("egs", [P, 3, P])
        egk = eb("egk", [P, 3, P])
        route = ctx.enter_context(ExitStack())

        def rb(name, shape, dt=F32):
            return route.enter_context(nc.sbuf_tensor(name, shape, dt))

        sc = rb("sc", [P, TT, 2 * PH * NK])
        st = rb("st", [P, 2 * PH, NK])
        st2 = rb("st2", [P, 2, NK])
        v16 = rb("v16", [P, PH, 2, TOP])
        i16 = rb("i16", [P, PH, 2, TOP], U32)
        i16f = rb("i16f", [P, PH, 2, TOP])
        cand = rb("cand", [P, PH // 2, TOP, TOP])
        cand2 = rb("cand2", [P, TOP * TOP])
        vs = rb("vs", [P, PH, TOP])
        ic = rb("ic", [P, PH, TOP], U32)
        ab = rb("ab", [P, 2, PH, TOP], U32)
        abf = rb("abf", [P, 2, PH, TOP])
        eq = rb("eq", [P, PH // 2, TOP, TOP])
        vd = rb("vd", [P, PH, TOP])
        vsum = rb("vsum", [P, PH])
        vrec = rb("vrec", [P, PH])
        route.close()
        gates = ctx.enter_context(ExitStack())

        def rb(name, shape, dt=F32):
            return gates.enter_context(nc.sbuf_tensor(name, shape, dt))

        egT = rb("egT", [P, 3, P])
        key_t = rb("key_t", [P, 2, P], BF16)
        gate_t = rb("gate_t", [P, 3, P], BF16)
        gleft = rb("gleft", [P, P])
        iota4 = rb("iota4", [P, NK, UT], BF16)
        eq1 = rb("eq1", [P, 2, NK, UT], BF16)
        oh2 = rb("oh2", [P, URING, NK, UT], BF16)
        oh1 = rb("oh1", [P, URING, 3, NK, UT], BF16)
        gst = rb("gst", [P, 2, NK, CHUNK])
        gates.close()

        hq = sb("hq", [P, 2, GT, S])
        before_gst = 3 * P * 4 + 5 * P * 2 + P * 4 + (3 + 4 * URING) * NK * UT * 2
        sb("gap", [P, (before_gst - 2 * GT * S * 4) // 4])
        gq = sb("gq", [P, 2, S // CHUNK, GW])
        chi = sb("chi", [P, 4, S], F32R)
        clo = sb("clo", [P, 4, S], F32R)
        cf = qp
        sg = cf
        ov = hout

        p_in, col_in, row_in, key_in = (sem(n) for n in ("p_in", "col_in", "row_in", "key_in"))
        x_in = [sem(f"x_in{t}") for t in range(TT)]
        w_in = [sem(f"w_in{i}") for i in range(RING)]
        consts = sem("consts")
        qgain_done = sem("qgain_done")
        hi_done, lo_done = sem("hi_done"), sem("lo_done")
        mm_done = sem("mm_done")
        p_hi_done, p_lo_done = sem("p_hi_done"), sem("p_lo_done")
        pp_act, pp_dve = sem("pp_act"), sem("pp_dve")
        NORMS = ("x", "y", "h1", "h2")
        sq_done = {n: sem("sq_" + n) for n in NORMS}
        ms_done = {n: sem("ms_" + n) for n in NORMS}
        sd_done = {n: sem("sd_" + n) for n in NORMS}
        rs_done = {n: sem("rs_" + n) for n in NORMS}
        diag_done = {n: sem("diag_" + n) for n in NORMS}
        tr_done = {n: sem("tr_" + n) for n in NORMS}
        xf_done = {n: sem("xf_" + n) for n in NORMS}
        nhi_done = {n: sem("nhi_" + n) for n in NORMS}
        nlo_done = {n: sem("nlo_" + n) for n in NORMS}
        sig_done, glu_done, conv_done = sem("sig_done"), sem("glu_done"), sem("conv_done")
        f_act, negf_done, f3_done = sem("f_act"), sem("negf_done"), sem("f3_done")
        sqk_done, qkraw_done, qk_sum, rt_done, rr_done, r3_done, qk_rms, qk_done = (
            sem(n) for n in ("sqk_done", "qkraw_done", "qk_sum", "rt_done", "rr_done", "r3_done", "qk_rms",
                             "qk_done"))
        vT_done, v_tr, vt_done = sem("vT_done"), sem("v_tr"), sem("vt_done")
        logits, max_done, exp_done, pT_tr, pT_done, o_done, rden_done, att_done = (
            sem(n) for n in ("logits", "max_done", "exp_done", "pT_tr", "pT_done", "o_done", "rden_done",
                             "att_done"))
        cy_tr, ln_stat, ln_mean, ln_sub, lsd_done, lrs_done, ln_gain, ln_out, csg_done, yc_done = (
            sem(n) for n in ("cy_tr", "ln_stat", "ln_mean", "ln_sub", "lsd_done", "lrs_done", "ln_gain", "ln_out",
                             "csg_done", "yc_done"))
        h1_done, h2_done = sem("h1_done"), sem("h2_done")
        u_free = sem("u_free")
        qp_done, sc_mm, sc_done = sem("qp_done"), sem("sc_mm"), sem("sc_done")
        h_stored = [sem(f"h_stored{i}") for i in range(RING)]
        st_done, st_used, rt_a, vd_done, vexp_done, egb_done = (
            sem(n) for n in ("st_done", "st_used", "routing_steps", "vd_done", "vexp_done", "egb_done"))
        egs_done, eg_tr, egT_done, parts_done = (
            sem(n) for n in ("egs_done", "eg_tr", "egT_done", "parts_done"))
        iota4_done, eq1_done = sem("iota4_done"), sem("eq1_done")
        oh_done, g_mm, g_out = (sem(n) for n in ("oh_done", "g_mm", "g_out"))
        g_stored = [sem("g_stored0"), sem("g_stored1")]
        hq_in, gq_in = [sem("hq_in0"), sem("hq_in1")], [sem("gq_in0"), sem("gq_in1")]
        cf_done, chi_done, clo_done = sem("cf_done"), sem("chi_done"), sem("clo_done")
        sg_done, sgp_pre, ov_done = sem("sg_done"), sem("sgp_pre"), sem("ov_done")
        out_done = [sem(f"out_done{i}") for i in range(4)]

        def wait(e, sm, value, g=None, per=STEP):
            e.wait_ge(sm, value if g is None else g * per + value)

        def turn(n, g, per=STEP):
            return n if g is None else g * per + n

        def split_hi(act, s, g=None):
            if s >= END:
                return
            wait(act, w_in[slot(s)], 16 * (s // RING + 1), g, 16 * STEP // RING)
            if s >= RING:
                wait(act, mm_done, s - RING + 1, g)
            act.activation(whi[:, slot(s)], raw[:, slot(s)], ACT.Copy).then_inc(hi_done, 1)

        def split_lo(dve, s, g=None):
            if s >= END:
                return
            wait(dve, hi_done, s + 1, g)
            dve.tensor_tensor(wlo[:, slot(s)], raw[:, slot(s)], whi[:, slot(s)], ALU.subtract).then_inc(lo_done, 1)

        def u_tile(pe, s, bank, g=None):
            wait(pe, lo_done, s + 1, g)
            wh = whi[:, slot(s)].rearrange("p (k c) -> p k c", k=KC)
            wl = wlo[:, slot(s)].rearrange("p (k c) -> p k c", k=KC)
            for k in range(KC):
                pe.matmul(ps[:, bank], wl[:, k], ahi[:, k], start=(k == 0), stop=False)
                pe.matmul(ps[:, bank], wh[:, k], alo[:, k], start=False, stop=False)
                last = pe.matmul(ps[:, bank], wh[:, k], ahi[:, k], start=False, stop=(k == KC - 1))
            last.then_inc(mm_done, 1)

        def v_tile(pe, s, a_hi, a_lo, first, final, g=None):
            wait(pe, lo_done, s + 1, g)
            for t in ((1, 2, 3, 0) if s == EV and first else range(TT)):
                if s == EV and first and t == 0:
                    pe.wait_ge(u_free, 2 * PH + NK)
                tok = slice(t * P, (t + 1) * P)
                for n, (a, w) in enumerate(((a_lo, whi), (a_hi, wlo), (a_hi, whi))):
                    for half in range(2):
                        last = pe.matmul(ps[:, 2 * t + half], a[:, tok], w[:, slot(s), half * S:(half + 1) * S],
                                         start=(first and n == 0), stop=(final and n == 2))
            last.then_inc(mm_done, 1)

        def norm_src(name, t, g):
            if name == "y":
                return (att, yc)[g][:, t]
            return xs[:, t]

        def groups(name):
            return 2 if name == "y" else 1

        def width(name):
            return D // groups(name)

        def norm_act_squares(act, name, t):
            n = NORMS.index(name)
            for g in range(groups(name)):
                act.activation(junk[:, g * width(name):(g + 1) * width(name)], norm_src(name, t, g), ACT.Square,
                               accum_out=ss[:, n, t, g:g + 1]).then_inc(sq_done[name], 1)

        def norm_act_root(act, name, t):
            n, G = NORMS.index(name), groups(name)
            act.wait_ge(ms_done[name], t + 1)
            act.activation(sd[:, n, t, :G], ms[:, n, t, :G], ACT.Sqrt).then_inc(sd_done[name], 1)

        def norm_dve_mean(dve, name, t):
            n, G = NORMS.index(name), groups(name)
            dve.wait_ge(sq_done[name], G * (t + 1))
            dve.tensor_scalar(ms[:, n, t, :G], ss[:, n, t, :G], 1.0 / width(name), EPS, ALU.mult,
                              ALU.add).then_inc(ms_done[name], 1)

        def norm_dve_diag(dve, name, t):
            n, G = NORMS.index(name), groups(name)
            dve.wait_ge(sd_done[name], t + 1)
            dve.reciprocal(rs[:, n, t, :G], sd[:, n, t, :G]).then_inc(rs_done[name], 1)
            dve.wait_ge(rs_done[name], t + 1)
            for g in range(G):
                dve.tensor_scalar(diag[:, t, g], ident[:], rs[:, n, t, g:g + 1], None,
                                  ALU.mult).then_inc(diag_done[name], 1)

        def norm_pe(pe, name, t):
            G = groups(name)
            for b in range(2):
                g = b if G == 2 else 0
                pe.wait_ge(diag_done[name], G * t + g + 1)
                for c in range(4):
                    col = c if G == 2 else 4 * b + c
                    last = pe.matmul(ps[:, 2 * t + b, c * P:(c + 1) * P],
                                     norm_src(name, t, g)[:, col * P:(col + 1) * P], diag[:, t, g],
                                     start=True, stop=True)
                last.then_inc(tr_done[name], 1)

        GAIN = {"x": C_LNMIX, "y": C_YG, "h1": C_LNFFN, "h2": C_LNPL}

        def norm_dst(buf, t, b):
            return buf[:, 4 * b:4 * b + 4, t * P:(t + 1) * P]

        def norm_dve_gain(dve, name, n):
            t, b = n // 2, n % 2
            dve.wait_ge(tr_done[name], n + 1)
            if n >= 2:
                dve.wait_ge(nlo_done[name], n - 1)
            g0 = GAIN[name] + 4 * b
            dve.tensor_tensor(xf[:, n % 2].rearrange("p (c t) -> p c t", c=4),
                              ps[:, n].rearrange("p (c t) -> p c t", c=4),
                              colc[:, g0:g0 + 4].unsqueeze(2).broadcast_to([P, 4, P]),
                              ALU.mult).then_inc(xf_done[name], 1)

        def norm_act_hi(act, name, n):
            act.wait_ge(xf_done[name], n + 1)
            act.activation(norm_dst(ahi, n // 2, n % 2), xf[:, n % 2].rearrange("p (c t) -> p c t", c=4),
                           ACT.Copy).then_inc(nhi_done[name], 1)

        def norm_dve_lo(dve, name, n):
            dve.wait_ge(nhi_done[name], n + 1)
            dve.tensor_tensor(norm_dst(alo, n // 2, n % 2), xf[:, n % 2].rearrange("p (c t) -> p c t", c=4),
                              norm_dst(ahi, n // 2, n % 2), ALU.subtract).then_inc(nlo_done[name], 1)

        def norm_dve_split(dve, name):
            for n in range(2 * TT + 1):
                if n < 2 * TT:
                    norm_dve_gain(dve, name, n)
                if n >= 1:
                    norm_dve_lo(dve, name, n - 1)

        LN_AT = 20
        HEADS = [(q, h) for q in range(TT) for h in range(H)]

        def units(j):
            return [(j - 4) * 4 + i for i in range(4)] if 4 <= j < 4 + UNITS // 4 else []

        block = ctx.enter_context(nc.Block())

        @block.sync
        def _(sp):
            def load(s, g=None):
                if s >= END:
                    return
                if s >= RING:
                    wait(sp, lo_done, s - RING + 1, g)
                sp.dma_start(raw[:, slot(s)], stream[turn(s, g)]).then_inc(w_in[slot(s)], 16)

            sp.dma_start(p_raw[:], pT).then_inc(p_in, 16)
            load(0)
            load(1)
            for t in range(TT):
                sp.dma_start(xs[:, t], x[t * P:(t + 1) * P, :]).then_inc(x_in[t], 16)
            sp.dma_start(colc[:], cols).then_inc(col_in, 16)
            sp.dma_start(lnrows[:], rows).then_inc(row_in, 16)
            for s in range(2, EU):
                load(s)
                if s == WO + 3:
                    sp.wait_ge(nlo_done["y"], 2 * TT)
                    sp.dma_start(kT[:], keysT).then_inc(key_in, 16)
            with sp.Fori(0, NK // STEP) as g:
                for j in range(STEP):
                    load(EU + j, g)

            def load_group(n, g=None):
                b = n % 2
                if g is None:
                    h_src, g_src = act_dram[GT * n:GT * n + GT], gate_dram[:, :, n * GW:(n + 1) * GW]
                else:
                    h_src = act_dram[bass.ds(g * STEP + GT * n, GT)]
                    g_src = gate_dram[:, :, bass.ds(g * (STEP * CHUNK) + n * GW, GW)]
                sp.dma_start(hq[:, b], h_src.rearrange("a p t -> p a t")).then_inc(hq_in[b], 16)
                sp.dma_start(gq[:, b], g_src.rearrange("c p n -> p c n")).then_inc(gq_in[b], 16)

            for s in range(EV, EV + RING - 1):
                load(s)
            for i in range(RING):
                sp.wait_ge(h_stored[i], 16 * 2 * GT // RING)
            for b in range(2):
                sp.wait_ge(g_stored[b], 16 * S // CHUNK // 2)
            sp.wait_ge(g_mm, UNITS * TT)
            load_group(0)
            load_group(1)
            load(EV + RING - 1)
            for i in range(RING):
                sp.wait_ge(h_stored[i], 16 * NK // RING)
            with sp.Fori(0, NK // STEP - 1) as g:
                for j in range(STEP):
                    load(EV + RING + j, g)
                    if j % GT == GT - 1:
                        wait(sp, cf_done, j + 1, g)
                        load_group(2 + j // GT, g)
            for s in range(EV + NK - STEP + RING, END):
                load(s)
                m = s - EV - RING
                if m % GT == GT - 1 and m // GT + 2 < NK // GT:
                    sp.wait_ge(cf_done, m + 1)
                    load_group(2 + m // GT)
            for n in range(2 * TT):
                t, half = n // 2, n % 2
                sp.wait_ge(ov_done, n + 1)
                sp.dma_start(out[t * P:(t + 1) * P, half * S:(half + 1) * S], ov[:, n % 4]).then_inc(out_done[n % 4], 16)
            for i in range(4):
                sp.wait_ge(out_done[i], 16 * 2 * TT // 4)

        @block.gpsimd
        def _(pool):
            n = [0]

            def step(ins):
                ins.then_inc(consts, 1)
                n[0] += 1
                if n[0] < N_CONSTS:
                    pool.wait_ge(consts, n[0])

            step(pool.memset(ident[:], 0.0))
            step(pool.affine_select(out=ident[:], in_=ident[:], compare_op=ALU.not_equal, fill=1.0, base=0,
                                    pattern=[[-1, P]], channel_multiplier=1))
            step(pool.memset(epsc[:, 0:1], EPS))
            step(pool.memset(epsc[:, 1:2], LN_EPS))
            step(pool.memset(glu[:, :, 0:CW - 1], 0.0))
            step(pool.memset(blk[:], 0.0))
            for i in range(2):
                step(pool.affine_select(out=blk[i * DH:(i + 1) * DH], in_=blk[i * DH:(i + 1) * DH],
                                        compare_op=ALU.not_equal, fill=1.0, base=-i,
                                        pattern=[[-2, 2 * CC], [1, 2 * H]], channel_multiplier=0))
            step(pool.memset(negmask[:], 0.0))
            step(pool.affine_select(out=negmask[:], in_=negmask[:], compare_op=ALU.is_ge, fill=NEG, base=0,
                                    pattern=[[-1, P]], channel_multiplier=1))
            step(pool.tensor_copy(identb[:], ident[:]))
            step(pool.memset(self_[:], 0.0))
            step(pool.memset(selq[:], 0.0))
            step(pool.memset(f3[:], 0.0))
            step(pool.memset(r3[:], 0.0))
            step(pool.memset(vt[:, :, DA:], 0.0))
            for base in (0, 32, 64):
                step(pool.affine_select(out=self_[base:base + 32], in_=self_[base:base + 32],
                                        compare_op=ALU.not_equal, fill=1.0, base=0,
                                        pattern=[[-1, H], [0, P]], channel_multiplier=1))
                for i in range(2):
                    part = selq[base:base + 32, :, i * DH:(i + 1) * DH]
                    step(pool.affine_select(out=part, in_=part, compare_op=ALU.not_equal, fill=1.0, base=-i,
                                            pattern=[[-2, 2 * CC], [0, DH]], channel_multiplier=1))
            step(pool.iota(iota[:], pattern=[[1, P]], base=0, channel_multiplier=0,
                           allow_small_or_imprecise_dtypes=True))
            assert n[0] == N_CONSTS

        @block.scalar
        def _(act):
            def v_copy(n):
                act.wait_ge(v_tr, n + 1)
                act.activation(vt[:, :, n * P:(n + 1) * P], ps[:, 4 + n % 2].rearrange("p (t c) -> p t c", t=TT),
                               ACT.Copy).then_inc(vt_done, 1)

            act.wait_ge(p_in, 16)
            act.activation(p_hi[:], p_raw[:], ACT.Copy).then_inc(p_hi_done, 1)
            for s in range(2):
                split_hi(act, s)
            for t in range(TT):
                act.wait_ge(x_in[t], 16)
                if t >= 1:
                    act.wait_ge(sq_done["x"], t)
                norm_act_squares(act, "x", t)
            for t in range(TT):
                norm_act_root(act, "x", t)
            for s in range(2, RING):
                split_hi(act, s)
            act.wait_ge(mm_done, PROJ + 2)
            for b in range(4):
                act.activation(pp[:, b // 2, (b % 2) * S:(b % 2 + 1) * S], ps[:, b], ACT.Copy).then_inc(pp_act, 1)
            for s in range(RING, GLU + LEAD):
                split_hi(act, s)
            act.wait_ge(col_in, 16)
            for n in range(2 * TT):
                norm_act_hi(act, "x", n)
            act.wait_ge(consts, N_CONSTS)
            for s in range(GLU, WO):
                split_hi(act, s + LEAD)
                if s < FG:
                    if (s - GLU) % 2 == 0:
                        c = (s - GLU) // 2
                        act.wait_ge(mm_done, s + 1)
                        if c >= 2:
                            act.wait_ge(glu_done, c - 1)
                        act.activation(sig[:, c % 2], ps[:, 0], ACT.Sigmoid).then_inc(sig_done, 1)
                elif s == FG:
                    act.wait_ge(mm_done, s + 1)
                    act.activation(fz[:, 0], ps[0:H, 0], ACT.Identity,
                                   bias=colc[0:H, C_BF:C_BF + 1]).then_inc(f_act, 1)
                    act.wait_ge(f_act, 1)
                    act.activation(fz[:, 1], fz[:, 0], ACT.Abs).then_inc(f_act, 1)
                    act.wait_ge(f_act, 2)
                    act.activation(fz[:, 2], fz[:, 1], ACT.Exp, scale=-1.0).then_inc(f_act, 1)
                    act.wait_ge(f_act, 3)
                    act.activation(fz[:, 3], fz[:, 2], ACT.Ln, bias=1.0).then_inc(f_act, 1)
                elif s < VV:
                    n = s - QK
                    act.wait_ge(mm_done, s + 1)
                    if n >= 2:
                        act.wait_ge(qk_sum, n - 1)
                    act.activation(sq[:, n % 2], ps[:, s % 2], ACT.Square).then_inc(sqk_done, 1)
                    act.activation(qk[:, n], ps[:, s % 2], ACT.Copy).then_inc(qkraw_done, 1)
                else:
                    n = s - VV
                    if n == 0:
                        act.wait_ge(qk_sum, 2 * CC)
                        act.activation(rt[:], ps[0:2 * H, 2], ACT.Sqrt, bias=epsc[0:2 * H, 0:1],
                                       scale=1.0 / DH).then_inc(rt_done, 1)
                    act.wait_ge(mm_done, s + 1)
                    if n >= 2:
                        act.wait_ge(v_tr, n - 1)
                    act.activation(vT[:, n % 2], ps[:, s % 2], ACT.Copy).then_inc(vT_done, 1)
                    if n >= 1:
                        v_copy(n - 1)
            v_copy(CC - 1)
            for i in range(len(HEADS) + 1):
                if i == LN_AT + 5:
                    act.wait_ge(ln_mean, TT)
                    act.activation(lsd[:], mv[:, :, 1], ACT.Sqrt, bias=epsc[:, 1:2]).then_inc(lsd_done, 1)
                if i == LN_AT + 9:
                    for t in range(TT):
                        act.wait_ge(ln_out, t + 1)
                        if t >= 2:
                            act.wait_ge(yc_done, t - 1)
                        act.activation(csg[:, t % 2], yc[:, t], ACT.Sigmoid).then_inc(csg_done, 1)
                if i < len(HEADS):
                    q, h = HEADS[i]
                    n = (q + 1) * P
                    act.wait_ge(max_done, i + 1)
                    if i >= 3:
                        act.wait_ge(pT_tr, i - 2)
                    act.activation(pr[:, i % 3, :n], ps[:, 2 + i % 2, :n], ACT.Exp, bias=nmax[:, i:i + 1],
                                   accum_out=den[:, i:i + 1]).then_inc(exp_done, 1)
                if i >= 1:
                    q, h = HEADS[i - 1]
                    n = (q + 1) * P
                    act.wait_ge(pT_tr, i)
                    if i >= 3:
                        act.wait_ge(o_done, i - 2)
                    act.activation(pT_sb[:, (i - 1) % 2, :n], ps[:, 4 + (i - 1) % 2, :n],
                                   ACT.Copy).then_inc(pT_done, 1)
            for t in range(TT):
                act.wait_ge(att_done, 2 * t + 2)
                act.wait_ge(yc_done, t + 1)
                if t >= 1:
                    act.wait_ge(sq_done["y"], 2 * t)
                norm_act_squares(act, "y", t)
            for t in range(TT):
                norm_act_root(act, "y", t)
            act.wait_ge(mm_done, WO)
            for n in range(2 * TT):
                norm_act_hi(act, "y", n)
            for s in range(WO, WO + KC):
                split_hi(act, s + LEAD)
            for t in range(TT):
                act.wait_ge(h1_done, t + 1)
                if t >= 1:
                    act.wait_ge(sq_done["h1"], t)
                norm_act_squares(act, "h1", t)
            for t in range(TT):
                norm_act_root(act, "h1", t)
            for n in range(2 * TT):
                norm_act_hi(act, "h1", n)
            for s in range(PQ, EU + 1):
                n = s - PQ
                if s < EU:
                    split_hi(act, s + LEAD)
                    act.wait_ge(mm_done, s + 1)
                    if n >= 2:
                        act.wait_ge(sc_mm, n - 1)
                    act.activation(qp[:, n % 2], ps[:, s % 2], ACT.Copy).then_inc(u_free, 1)
                if n >= 1:
                    act.wait_ge(sc_mm, n)
                    act.activation(sc[:, :, (n - 1) * NK:n * NK],
                                   ps[:, 2 + (n - 1) % 2].rearrange("p (t k) -> p t k", t=TT),
                                   ACT.Copy).then_inc(sc_done, 1)

            def gelu(n, g=None):
                wait(act, mm_done, EU + n + 1, g)
                if n >= RING:
                    wait(act, h_stored[n % RING], 16 * (n // RING), g, 16 * STEP // RING)
                act.activation(hout[:, n % RING], ps[:, (EU + n) % 2], ACT.Gelu_apprx_tanh).then_inc(u_free, 1)
                wait(act, u_free, 2 * PH + n + 1, g)
                act.dma_start(act_dram[turn(n, g)], hout[:, n % RING]).then_inc(h_stored[n % RING], 16)

            def routing_turn(it, g=None):
                if it >= 1:
                    wait(act, st_used, it, g, 1)
                act.activation(st[:], sc[:, turn(it, g, 1)].rearrange("p (h k) -> p h k", k=NK),
                               ACT.Copy).then_inc(st_done, 1)
                for j in range(STEP):
                    split_hi(act, EU + it * STEP + j + LEAD, g)
                    gelu(it * STEP + j, g)
                wait(act, vd_done, it + 1, g, 1)
                act.activation(vd[:], vd[:], ACT.Exp).then_inc(vexp_done, 1)

            act.wait_ge(sc_done, 2 * PH)
            routing_turn(0)
            with act.Fori(0, TT - 1) as g:
                routing_turn(1, g)

            def gate_turn(it, g=None):
                for j in range(STEP):
                    if j == 1:
                        wait(act, egb_done, TT)
                        if it >= 1:
                            wait(act, eg_tr, it, g, 1)
                        act.activation(egs[:], egb[:, turn(it, g, 1)], ACT.Copy).then_inc(egs_done, 1)
                    split_hi(act, EU + (TT + it) * STEP + j + LEAD, g)
                    gelu((TT + it) * STEP + j, g)
                    if j == 2:
                        wait(act, eg_tr, it + 1, g, 1)
                        if it >= 1:
                            wait(act, parts_done, 6 * it, g, 6)
                        act.activation(egT[:], ps[:, 6, 0:3 * P].rearrange("p (n t) -> p n t", n=3),
                                       ACT.Copy).then_inc(egT_done, 1)
                    for u in units(j):
                        k = UNITS * it + u
                        buf = (u // UCHUNK) % 2
                        wait(act, g_mm, k + 1, g, UNITS)
                        if u % UCHUNK == 0 and k >= 2 * UCHUNK:
                            wait(act, g_stored[buf], 16 * (k // UCHUNK // 2), g, 16 * P // CHUNK // 2)
                        tok = (u % UCHUNK) * UT
                        act.activation(gst[:, buf, :, tok:tok + UT].rearrange("p e t -> p t e"),
                                       ps[:, 2 + u % 4].rearrange("p (t e) -> p t e", t=UT),
                                       ACT.Copy).then_inc(g_out, 1)
                        if u % UCHUNK == UCHUNK - 1:
                            wait(act, g_out, k + 1, g, UNITS)
                            act.dma_start(gate_dram[turn(k // UCHUNK, g, P // CHUNK)],
                                          gst[:, buf].rearrange("p e t -> p (e t)")).then_inc(g_stored[buf], 16)

            gate_turn(0)
            with act.Fori(0, TT - 1) as g:
                gate_turn(1, g)

            def coef_hi(m, g=None):
                if m >= NK:
                    return
                wait(act, cf_done, m + 1, g)
                if m >= 4:
                    wait(act, mm_done, EV + m - 3, g)
                act.activation(chi[:, m % 4], cf[:, m % 2], ACT.Copy).then_inc(chi_done, 1)

            def expert_v_turn(it, g=None):
                for j in range(STEP):
                    split_hi(act, EV + it * STEP + j + LEAD, g)
                    coef_hi(it * STEP + j + CLEAD, g)

            for b in range(2):
                act.wait_ge(g_stored[b], 16 * S // CHUNK // 2)
            for m in range(CLEAD):
                coef_hi(m)
            expert_v_turn(0)
            with act.Fori(0, NK // STEP - 2) as g:
                expert_v_turn(1, g)
            expert_v_turn(NK // STEP - 1)
            for t in range(TT):
                act.wait_ge(h2_done, t + 1)
                if t >= 1:
                    act.wait_ge(sq_done["h2"], t)
                norm_act_squares(act, "h2", t)
            for t in range(TT):
                norm_act_root(act, "h2", t)
            for n in range(2 * TT):
                norm_act_hi(act, "h2", n)
            for s in range(GA, END):
                split_hi(act, s + LEAD)
            act.wait_ge(mm_done, END)
            for n in range(2 * TT):
                if n >= 2:
                    act.wait_ge(ov_done, n - 1)
                act.activation(sg[:, n % 2], ps[:, n], ACT.Sigmoid).then_inc(sg_done, 1)

        @block.vector
        def _(dve):
            dve.wait_ge(p_hi_done, 1)
            dve.tensor_tensor(p_lo[:], p_raw[:], p_hi[:], ALU.subtract).then_inc(p_lo_done, 1)
            for s in range(2):
                split_lo(dve, s)
            for t in range(TT):
                norm_dve_mean(dve, "x", t)
            dve.wait_ge(consts, N_CONSTS)
            for t in range(TT):
                norm_dve_diag(dve, "x", t)
            for s in range(2, RING):
                split_lo(dve, s)
            dve.wait_ge(mm_done, PROJ + 2)
            for b in range(4, 8):
                dve.tensor_copy(pp[:, b // 2, (b % 2) * S:(b % 2 + 1) * S], ps[:, b]).then_inc(pp_dve, 1)
            for s in range(RING, GLU + LEAD):
                split_lo(dve, s)
            dve.wait_ge(col_in, 16)
            dve.tensor_scalar(qgain[:], colc[:, C_QN:C_QN + 1], DH ** -0.5, None, ALU.mult).then_inc(qgain_done, 1)
            norm_dve_split(dve, "x")

            conv = [0]

            def conv_taps(count, channels):
                for _ in range(count):
                    n = conv[0]
                    if n >= channels * CW:
                        return
                    conv[0] += 1
                    c, w = n // CW, n % CW
                    src = glu[:, c, w:w + S]
                    tap = colc[:, C_CW + c * CW + w:C_CW + c * CW + w + 1]
                    if w == 0:
                        dve.wait_ge(glu_done, c + 1)
                        dve.tensor_scalar(cy[:, c], src, tap, colc[:, C_CB + c:C_CB + c + 1], ALU.mult,
                                          ALU.add).then_inc(conv_done, 1)
                    else:
                        dve.wait_ge(conv_done, n)
                        dve.scalar_tensor_tensor(cy[:, c], src, tap, cy[:, c], ALU.mult,
                                                 ALU.add).then_inc(conv_done, 1)

            def three_parts(dst, a, rows_n, left, done):
                dve.tensor_copy(dst[0:rows_n], a).then_inc(done, 1)
                dve.wait_ge(done, 1)
                dve.tensor_tensor(left, a, dst[0:rows_n], ALU.subtract).then_inc(done, 1)
                dve.wait_ge(done, 2)
                dve.tensor_copy(mid[0:rows_n], left).then_inc(done, 1)
                dve.wait_ge(done, 3)
                dve.tensor_copy(dst[32:32 + rows_n], mid[0:rows_n]).then_inc(done, 1)
                dve.tensor_tensor(left, left, mid[0:rows_n], ALU.subtract).then_inc(done, 1)
                dve.wait_ge(done, 5)
                dve.tensor_copy(dst[64:64 + rows_n], left).then_inc(done, 1)

            def qk_norm(n):
                dve.wait_ge(qk_rms, n + 1)
                dve.wait_ge(qgain_done, 1)
                gain = colc[:, C_KN:C_KN + 1] if n % 2 else qgain[:]
                dve.scalar_tensor_tensor(qk[:, n], qk[:, n], gain, ps[:, 2 + n % 2], ALU.mult,
                                         ALU.mult).then_inc(qk_done, 1)

            for s in range(GLU, WO):
                split_lo(dve, s + LEAD)
                if s < FG and (s - GLU) % 2 == 1:
                    c = (s - GLU) // 2
                    dve.wait_ge(mm_done, s + 1)
                    dve.wait_ge(sig_done, c + 1)
                    dve.tensor_tensor(glu[:, c, CW - 1:], ps[:, 1], sig[:, c % 2], ALU.mult).then_inc(glu_done, 1)
                if s == FG + 1:
                    dve.wait_ge(f_act, 4)
                    dve.scalar_tensor_tensor(fz[:, 1], fz[:, 0], 0.0, fz[:, 3], ALU.min,
                                             ALU.subtract).then_inc(negf_done, 1)
                    dve.wait_ge(negf_done, 1)
                    dve.tensor_scalar(fz[:, 2], fz[:, 1], -1.0, None, ALU.mult).then_inc(negf_done, 1)
                    dve.wait_ge(negf_done, 2)
                    dve.tensor_tensor_scan(negf[:, 0], fz[:, 2], fz[:, 2], 0.0, ALU.add,
                                           ALU.bypass).then_inc(negf_done, 1)
                    dve.wait_ge(negf_done, 3)
                    three_parts(f3, negf[:, 0], H, negf[:, 1], f3_done)
                if s == VV + 1:
                    dve.wait_ge(rt_done, 1)
                    dve.reciprocal(rr[:, 0], rt[:]).then_inc(rr_done, 1)
                    dve.wait_ge(rr_done, 1)
                    three_parts(r3, rr[:, 0], 2 * H, rr[:, 1], r3_done)
                if s == VV + 2:
                    for n in range(2 * CC):
                        qk_norm(n)
                if s > GLU + 1:
                    conv_taps(4 if s < VV else 2, max(0, min(CC, (s - GLU) // 2)))

            def heads_out(q, b):
                k, hs = 2 * q + b, slice(q * H + 4 * b, q * H + 4 * b + 4)
                dve.wait_ge(exp_done, hs.stop)
                dve.reciprocal(rden[:, hs], den[:, hs]).then_inc(rden_done, 1)
                dve.wait_ge(rden_done, k + 1)
                dve.wait_ge(o_done, hs.stop)
                dve.tensor_tensor(att[:, q, 4 * b * DH:4 * (b + 1) * DH].rearrange("p (h d) -> p h d", h=4),
                                  ps[:, 6 + b, 0:4 * DH].rearrange("p (h d) -> p h d", h=4),
                                  rden[:, hs].unsqueeze(2).broadcast_to([P, 4, DH]),
                                  ALU.mult).then_inc(att_done, 1)

            def ln_center(t):
                dve.wait_ge(cy_tr, t + 1)
                dve.bn_stats(bn[:, t], ps[:, t % 2]).then_inc(ln_stat, 1)
                dve.wait_ge(ln_stat, t + 1)
                dve.bn_aggr(mv[:, t], bn[:, t]).then_inc(ln_mean, 1)
                dve.wait_ge(ln_mean, t + 1)
                dve.tensor_scalar(yc[:, t], ps[:, t % 2], mv[:, t, 0:1], None, ALU.subtract).then_inc(ln_sub, 1)

            def ln_scale(t):
                if t == 0:
                    dve.wait_ge(lsd_done, 1)
                    dve.reciprocal(lrs[:], lsd[:]).then_inc(lrs_done, 1)
                    dve.wait_ge(lrs_done, 1)
                    dve.wait_ge(row_in, 16)
                dve.scalar_tensor_tensor(yc[:, t], yc[:, t], lrs[:, t:t + 1], lnrows[:, 0], ALU.mult,
                                         ALU.mult).then_inc(ln_gain, 1)
                dve.wait_ge(ln_gain, t + 1)
                dve.tensor_tensor(yc[:, t], yc[:, t], lnrows[:, 1], ALU.add).then_inc(ln_out, 1)

            def swish(t):
                dve.wait_ge(csg_done, t + 1)
                dve.tensor_tensor(yc[:, t], yc[:, t], csg[:, t % 2], ALU.mult).then_inc(yc_done, 1)

            for i in range(len(HEADS) + 2):
                if i < len(HEADS):
                    q, h = HEADS[i]
                    n = (q + 1) * P
                    dve.wait_ge(logits, i + 1)
                    dve.tensor_reduce(nmax[:, i:i + 1], ps[:, 2 + i % 2, :n], AX.X, ALU.max,
                                      negate=True).then_inc(max_done, 1)
                if i >= 2 and (i - 2) % 4 == 3:
                    heads_out((i - 2) // H, (i - 2) // 4 % 2)
                if i < LN_AT:
                    conv_taps(CC * CW if i == LN_AT - 1 else 3, CC)
                elif i < LN_AT + TT:
                    ln_center(i - LN_AT)
                elif LN_AT + 5 <= i < LN_AT + 5 + TT:
                    ln_scale(i - LN_AT - 5)
                elif i in (LN_AT + 9, LN_AT + 10):
                    for t in (0, 1) if i == LN_AT + 9 else (2, 3):
                        swish(t)
            for t in range(TT):
                norm_dve_mean(dve, "y", t)
            for t in range(TT):
                norm_dve_diag(dve, "y", t)
            norm_dve_split(dve, "y")
            for s in range(WO, WO + KC):
                split_lo(dve, s + LEAD)
            dve.wait_ge(mm_done, WO + KC)
            for t in range(TT):
                dve.tensor_tensor(xs[:, t].rearrange("p (b n) -> p b n", b=2), ps[:, 2 * t:2 * t + 2],
                                  xs[:, t].rearrange("p (b n) -> p b n", b=2), ALU.add).then_inc(h1_done, 1)
            for t in range(TT):
                norm_dve_mean(dve, "h1", t)
            for t in range(TT):
                norm_dve_diag(dve, "h1", t)
            norm_dve_split(dve, "h1")
            for s in range(PQ, EU):
                split_lo(dve, s + LEAD)
            dve.wait_ge(sc_done, 2 * PH)

            def routing_turn(it, g=None):
                n = [0]

                def step(ins):
                    n[0] += 1
                    ins.then_inc(rt_a, 1)
                    return n[0]

                def need(k):
                    dve.wait_ge(rt_a, k)

                def top16(top_at, idx_at, src, rest):
                    k = [step(dve.max(top_at(r)[:, 0:8], src(r))) for r in range(len(rest))]
                    need(k[-1])
                    k = [step(dve.match_replace(rest[r], top_at(r)[:, 0:8], src(r), NEG)) for r in range(len(rest))]
                    for r in range(len(rest)):
                        step(dve.max_index(idx_at(r)[:, 0:8], top_at(r)[:, 0:8], src(r)))
                    need(k[-1])
                    k = [step(dve.max(top_at(r)[:, 8:16], rest[r])) for r in range(len(rest))]
                    need(k[-1])
                    for r in range(len(rest)):
                        last = step(dve.max_index(idx_at(r)[:, 8:16], top_at(r)[:, 8:16], rest[r]))
                    return last

                def candidates(h0):
                    shape = [P, PH // 2, TOP, TOP]
                    return step(dve.tensor_tensor(
                        cand[:], v16[:, h0:h0 + 4, 0].unsqueeze(3).broadcast_to(shape),
                        v16[:, h0:h0 + 4, 1].unsqueeze(2).broadcast_to(shape), ALU.add))

                def resolve(h0):
                    hs = slice(h0, h0 + 4)
                    shape = [P, PH // 2, TOP, TOP]
                    step(dve.tensor_scalar(ab[:, 0, hs], ic[:, hs], 4, None, ALU.logical_shift_right))
                    k = step(dve.tensor_scalar(ab[:, 1, hs], ic[:, hs], 15, None, ALU.bitwise_and))
                    need(k)
                    k = step(dve.tensor_copy(abf[:, :, hs], ab[:, :, hs]))
                    for half in range(2):
                        need(k)
                        k = step(dve.tensor_tensor(
                            eq[:], abf[:, half, hs].unsqueeze(3).broadcast_to(shape),
                            iota[:, 0:TOP].unsqueeze(1).unsqueeze(1).broadcast_to(shape), ALU.is_equal))
                        need(k)
                        k = step(dve.tensor_tensor(
                            eq[:], eq[:], i16f[:, hs, half].unsqueeze(2).broadcast_to(shape), ALU.mult))
                        need(k)
                        k = step(dve.tensor_reduce(
                            egk[:, half, h0 * TOP:(h0 + 4) * TOP].rearrange("p (h j) -> p h j", h=4), eq[:],
                            AX.X, ALU.add))
                    return k

                wait(dve, st_done, it + 1, g, 1)
                if it >= 1:
                    wait(dve, egb_done, it, g, 1)
                for j in range(STEP):
                    split_lo(dve, EU + it * STEP + j + LEAD, g)
                    if j < PH:
                        last = top16(lambda r: v16[:, j, r], lambda r: i16[:, j, r], lambda r: st[:, 2 * j + r],
                                     [st2[:, 0], st2[:, 1]])
                        if j == PH - 1:
                            need(last)
                            dve.tensor_copy(i16f[:], i16[:]).then_inc(st_used, 1)
                    else:
                        h = j - PH
                        if h == 0:
                            wait(dve, st_used, it + 1, g, 1)
                        if h % 4 == 0:
                            need(candidates(h))
                        last = top16(lambda r: vs[:, h], lambda r: ic[:, h],
                                     lambda r: cand[:, h % 4].rearrange("p a b -> p (a b)"), [cand2[:]])
                        if h == PH - 1:
                            need(last)
                            dve.tensor_tensor(vd[:], vs[:], vs[:, :, 0:1].broadcast_to([P, PH, TOP]),
                                              ALU.subtract).then_inc(vd_done, 1)
                        if h % 4 == 3:
                            need(last)
                            last = resolve(h - 3)
                wait(dve, vexp_done, it + 1, g, 1)
                k = step(dve.tensor_reduce(vsum[:], vd[:], AX.X, ALU.add))
                need(k)
                k = step(dve.reciprocal(vrec[:], vsum[:]))
                need(k)
                k = step(dve.tensor_tensor(egk[:, 2].rearrange("p (h j) -> p h j", h=PH), vd[:],
                                           vrec[:].unsqueeze(2).broadcast_to([P, PH, TOP]), ALU.mult))
                need(k)
                dve.sem_clear(rt_a)
                dve.tensor_copy(egb[:, turn(it, g, 1)], egk[:]).then_inc(egb_done, 1)

            routing_turn(0)
            with dve.Fori(0, TT - 1) as g:
                routing_turn(1, g)

            dve.wait_ge(egb_done, TT)
            dve.tensor_copy(iota4[:], iota[:].unsqueeze(2).broadcast_to([P, NK, UT])).then_inc(iota4_done, 1)
            dve.wait_ge(iota4_done, 1)

            def key_and_gate_parts(it, g):
                def step(k, ins):
                    ins.then_inc(parts_done, 1)
                    wait(dve, parts_done, 6 * it + k, g, 6)

                wait(dve, egT_done, it + 1, g, 1)
                if it >= 1:
                    wait(dve, oh_done, UNITS * it, g, UNITS)
                dve.tensor_copy(key_t[:], egT[:, 0:2]).then_inc(parts_done, 1)
                step(2, dve.tensor_copy(gate_t[:, 0], egT[:, 2]))
                step(3, dve.tensor_tensor(gleft[:], egT[:, 2], gate_t[:, 0], ALU.subtract))
                step(4, dve.tensor_copy(gate_t[:, 1], gleft[:]))
                step(5, dve.tensor_tensor(gleft[:], gleft[:], gate_t[:, 1], ALU.subtract))
                step(6, dve.tensor_copy(gate_t[:, 2], gleft[:]))

            def one_hot_rows(u, it, g):
                k = UNITS * it + u
                tok = slice(UT * u, UT * (u + 1))
                shape = [P, NK, UT]
                if k >= 2:
                    wait(dve, oh_done, k - 1, g, UNITS)
                dve.tensor_tensor(eq1[:, k % 2], iota4[:], key_t[:, 0, tok].unsqueeze(1).broadcast_to(shape),
                                  ALU.is_equal).then_inc(eq1_done, 1)
                if k >= URING:
                    wait(dve, g_mm, k - URING + 1, g, UNITS)
                dve.tensor_tensor(oh2[:, u % URING], iota4[:], key_t[:, 1, tok].unsqueeze(1).broadcast_to(shape),
                                  ALU.is_equal)
                wait(dve, eq1_done, k + 1, g, UNITS)
                dve.tensor_tensor(oh1[:, u % URING], eq1[:, k % 2].unsqueeze(1).broadcast_to([P, 3, NK, UT]),
                                  gate_t[:, :, tok].unsqueeze(2).broadcast_to([P, 3, NK, UT]),
                                  ALU.mult).then_inc(oh_done, 1)

            def gate_turn(it, g=None):
                for j in range(STEP):
                    split_lo(dve, EU + (TT + it) * STEP + j + LEAD, g)
                    if j == 3:
                        key_and_gate_parts(it, g)
                    for u in units(j + 1):
                        one_hot_rows(u, it, g)

            gate_turn(0)
            with dve.Fori(0, TT - 1) as g:
                gate_turn(1, g)

            def coef(m):
                b, e = (m // GT) % 2, m % GT
                return (hq[:, b, e].rearrange("p (c t) -> p c t", c=S // CHUNK),
                        gq[:, b, :, e * CHUNK:(e + 1) * CHUNK])

            def coef_make(m, g=None):
                if m >= NK:
                    return
                if m % GT == 0:
                    b, turns = (m // GT) % 2, STEP // GT // 2
                    wait(dve, hq_in[b], 16 * (m // GT // 2 + 1), g, 16 * turns)
                    wait(dve, gq_in[b], 16 * (m // GT // 2 + 1), g, 16 * turns)
                if m >= 2:
                    wait(dve, clo_done, m - 1, g)
                a, w = coef(m)
                dve.tensor_tensor(cf[:, m % 2].rearrange("p (c t) -> p c t", c=S // CHUNK), a, w,
                                  ALU.mult).then_inc(cf_done, 1)

            def coef_lo(m, g=None):
                if m >= NK:
                    return
                wait(dve, chi_done, m + 1, g)
                dve.tensor_tensor(clo[:, m % 4], cf[:, m % 2], chi[:, m % 4], ALU.subtract).then_inc(clo_done, 1)

            def expert_v_turn(it, g=None):
                for j in range(STEP):
                    split_lo(dve, EV + it * STEP + j + LEAD, g)
                    coef_make(it * STEP + j + CLEAD, g)
                    coef_lo(it * STEP + j + CLEAD, g)

            for b in range(2):
                dve.wait_ge(g_stored[b], 16 * S // CHUNK // 2)
            for m in range(CLEAD):
                coef_make(m)
                coef_lo(m)
            expert_v_turn(0)
            with dve.Fori(0, NK // STEP - 2) as g:
                expert_v_turn(1, g)
            expert_v_turn(NK // STEP - 1)

            dve.wait_ge(mm_done, GA)
            for t in range(TT):
                dve.tensor_tensor(xs[:, t].rearrange("p (b n) -> p b n", b=2), ps[:, 2 * t:2 * t + 2],
                                  xs[:, t].rearrange("p (b n) -> p b n", b=2), ALU.add).then_inc(h2_done, 1)
            for t in range(TT):
                norm_dve_mean(dve, "h2", t)
            for t in range(TT):
                norm_dve_diag(dve, "h2", t)
            norm_dve_split(dve, "h2")
            for s in range(GA, END):
                split_lo(dve, s + LEAD)
            for n in range(2 * TT):
                t, half = n // 2, n % 2
                part = slice(half * S, (half + 1) * S)
                dve.wait_ge(sg_done, n + 1)
                dve.tensor_tensor(sg[:, n % 2], sg[:, n % 2], pp[:, t, part], ALU.mult).then_inc(sgp_pre, 1)
                dve.wait_ge(sgp_pre, n + 1)
                if n >= 4:
                    dve.wait_ge(out_done[n % 4], 16 * (n // 4))
                dve.tensor_tensor(ov[:, n % 4], sg[:, n % 2], xs[:, t, part], ALU.add).then_inc(ov_done, 1)

        @block.tensor
        def _(pe):
            pe.wait_ge(p_lo_done, 1)
            for s in range(PROJ, GLU):
                v_tile(pe, s, p_hi[:, s - PROJ], p_lo[:, s - PROJ], s == PROJ, s == GLU - 1)
            pe.wait_ge(pp_act, 4)
            pe.wait_ge(pp_dve, 4)
            for t in range(TT):
                norm_pe(pe, "x", t)
            pe.wait_ge(nlo_done["x"], 2 * TT)

            def qk_squares(n):
                pe.wait_ge(sqk_done, n + 1)
                pe.matmul(ps[0:2 * H, 2], blk[:, n], sq[:, n % 2], start=(n == 0),
                          stop=(n == 2 * CC - 1)).then_inc(qk_sum, 1)

            def qk_spread(n):
                pe.wait_ge(r3_done, 6)
                if n == 0:
                    pe.wait_ge(rt_done, 1)
                if n >= 2:
                    pe.wait_ge(qk_done, n - 1)
                pe.matmul(ps[:, 2 + n % 2], selq[:, n], r3[:], start=True, stop=True).then_inc(qk_rms, 1)

            def v_transpose(n):
                pe.wait_ge(vT_done, n + 1)
                if n >= 2:
                    pe.wait_ge(vt_done, n - 1)
                for t in range(TT):
                    last = pe.transpose(ps[:, 4 + n % 2, t * P:(t + 1) * P], vT[:, n % 2, t * P:(t + 1) * P], ident[:])
                last.then_inc(v_tr, 1)

            def bank_wait(s):
                p = s - 2
                if p < GLU:
                    return
                if p < FG:
                    c = (p - GLU) // 2
                    pe.wait_ge(glu_done if (p - GLU) % 2 else sig_done, c + 1)
                elif p == FG:
                    pe.wait_ge(f_act, 1)
                elif p < VV:
                    pe.wait_ge(qkraw_done, p - QK + 1)
                else:
                    pe.wait_ge(vT_done, p - VV + 1)

            for s in range(GLU, WO):
                bank_wait(s)
                u_tile(pe, s, s % 2)
                if QK < s <= VV:
                    qk_squares(s - QK - 1)
                if s == VV + 2:
                    for n in range(2):
                        qk_spread(n)
                if s > VV:
                    v_transpose(s - VV - 1)
            for n in range(2, 2 * CC):
                qk_spread(n)
            v_transpose(CC - 1)

            def att_logits(i):
                q, h = HEADS[i]
                n, rows_h = (q + 1) * P, slice((h % 2) * DH, (h % 2 + 1) * DH)
                bank = ps[:, 2 + i % 2]
                if i >= 2:
                    pe.wait_ge(exp_done, i - 1)
                pe.matmul(bank[:, :n], qk[rows_h, 2 * (h // 2), q * P:(q + 1) * P], qk[rows_h, 2 * (h // 2) + 1, :n],
                          start=True, stop=False)
                pe.matmul(bank[:, :n], self_[:, h], f3[:, :n], start=False, stop=False)
                pe.matmul(bank[:, n - P:n], identb[:], negmask[:], start=False, stop=True).then_inc(logits, 1)

            def att_transpose(i):
                q, h = HEADS[i]
                pe.wait_ge(exp_done, i + 1)
                if i >= 2:
                    pe.wait_ge(pT_done, i - 1)
                for k in range(q + 1):
                    last = pe.transpose(ps[:, 4 + i % 2, k * P:(k + 1) * P], pr[:, i % 3, k * P:(k + 1) * P], ident[:])
                last.then_inc(pT_tr, 1)

            def att_values(i):
                q, h = HEADS[i]
                pe.wait_ge(pT_done, i + 1)
                if q >= 1 and h % 4 == 0:
                    pe.wait_ge(att_done, 2 * q - 1 + h // 4)
                for k in range(q + 1):
                    last = pe.matmul(ps[:, 6 + h // 4, h % 4 * DH:(h % 4 + 2) * DH],
                                     pT_sb[:, i % 2, k * P:(k + 1) * P], vt[:, k, h * DH:(h + 2) * DH],
                                     start=(k == 0), stop=(k == q))
                last.then_inc(o_done, 1)

            pe.wait_ge(qk_done, 2 * CC)
            pe.wait_ge(f3_done, 6)
            pe.wait_ge(vt_done, CC)
            for i in range(len(HEADS) + 2):
                if i < len(HEADS):
                    att_logits(i)
                if 1 <= i <= len(HEADS):
                    att_transpose(i - 1)
                if i >= 2:
                    att_values(i - 2)
                if LN_AT <= i < LN_AT + TT:
                    t = i - LN_AT
                    pe.wait_ge(conv_done, CC * CW)
                    if t >= 2:
                        pe.wait_ge(ln_sub, t - 1)
                    for c in range(CC):
                        last = pe.transpose(ps[:, t % 2, c * P:(c + 1) * P], cy[:, c, t * P:(t + 1) * P], ident[:])
                    last.then_inc(cy_tr, 1)
            pe.wait_ge(att_done, 2 * TT)
            for t in range(TT):
                norm_pe(pe, "y", t)
            pe.wait_ge(nlo_done["y"], 2 * TT)
            for s in range(WO, PQ):
                v_tile(pe, s, ahi[:, s - WO], alo[:, s - WO], s == WO, s == PQ - 1)
            for t in range(TT):
                norm_pe(pe, "h1", t)
            pe.wait_ge(nlo_done["h1"], 2 * TT)

            pe.wait_ge(key_in, 16)
            for s in range(PQ, EU + 1):
                n = s - PQ
                if s < EU:
                    if n >= 2:
                        pe.wait_ge(u_free, n - 1)
                    u_tile(pe, s, s % 2)
                if n >= 1:
                    m = n - 1
                    pe.wait_ge(u_free, m + 1)
                    if m >= 2:
                        pe.wait_ge(sc_done, m - 1)
                    for t in range(TT):
                        last = pe.matmul(ps[:, 2 + m % 2, t * NK:(t + 1) * NK], qp[:, m % 2, t * P:(t + 1) * P],
                                         kT[:, m % 2], start=True, stop=True)
                    last.then_inc(sc_mm, 1)

            def expert_u(n, g=None):
                wait(pe, u_free, 2 * PH + n - 1, g)
                u_tile(pe, EU + n, (EU + n) % 2, g)

            with pe.Fori(0, TT) as g:
                for j in range(STEP):
                    expert_u(j, g)

            def gate_turn(it, g=None):
                for j in range(STEP):
                    expert_u((TT + it) * STEP + j, g)
                    if j == 1:
                        wait(pe, egs_done, it + 1, g, 1)
                        if it >= 1:
                            wait(pe, egT_done, it, g, 1)
                        for i in range(3):
                            last = pe.transpose(ps[:, 6, i * P:(i + 1) * P], egs[:, i], ident[:])
                        last.then_inc(eg_tr, 1)
                    for u in units(j):
                        k = UNITS * it + u
                        wait(pe, oh_done, k + 1, g, UNITS)
                        if k >= 4:
                            wait(pe, g_out, k - 3, g, UNITS)
                        for t in range(UT):
                            for part in range(3):
                                last = pe.matmul(ps[:, 2 + u % 4, t * NK:(t + 1) * NK], oh2[:, u % URING, :, t],
                                                 oh1[:, u % URING, part, :, t], start=(part == 0), stop=(part == 2))
                        last.then_inc(g_mm, 1)

            gate_turn(0)
            with pe.Fori(0, TT - 1) as g:
                gate_turn(1, g)

            pe.wait_ge(g_out, UNITS * TT)

            def expert_v_turn(it, g=None):
                for j in range(STEP):
                    m = it * STEP + j
                    wait(pe, clo_done, m + 1, g)
                    v_tile(pe, EV + m, chi[:, m % 4], clo[:, m % 4], m == 0, m == NK - 1, g)

            expert_v_turn(0)
            with pe.Fori(0, NK // STEP - 2) as g:
                expert_v_turn(1, g)
            expert_v_turn(NK // STEP - 1)
            for t in range(TT):
                if t == 0:
                    pe.wait_ge(h2_done, TT)
                norm_pe(pe, "h2", t)
            pe.wait_ge(nlo_done["h2"], 2 * TT)
            for s in range(GA, END):
                v_tile(pe, s, ahi[:, s - GA], alo[:, s - GA], s == GA, s == END - 1)


def kernel(**inputs):
    import numpy as np
    import concourse.bacc as bacc
    from concourse.bass_utils import run_bass_kernel_spmd as run

    a = {k: np.asarray(v) for k, v in inputs.items()}
    depth, batch = a["ln_mix"].shape[0], a["x"].shape[0]
    assert depth == 1 and batch == 1 and a["x"].shape[1:] == (S, D)

    def k_major(w):
        return w.reshape(KC, P, P).transpose(1, 0, 2).reshape(P, D)

    w_in = a["w_in"][0]
    at = 3 * DA + H
    col = lambda c0: k_major(w_in[:, c0:c0 + P])
    stream = np.zeros((END, P, D), np.float32)
    stream[PROJ:GLU] = a["w_pl_proj"][0].reshape(-1, P, D)
    for c in range(CC):
        stream[GLU + 2 * c] = col(at + DA + c * P)
        stream[GLU + 2 * c + 1] = col(at + c * P)
        stream[QK + 2 * c] = col(c * P)
        stream[QK + 2 * c + 1] = col(DA + c * P)
        stream[VV + c] = col(2 * DA + c * P)
    stream[FG].reshape(P, KC, P)[:, :, :H] = w_in[:, 3 * DA:at].reshape(KC, P, H).transpose(1, 0, 2)
    stream[WO:PQ] = a["w_out"][0].reshape(KC, P, D)
    for m in range(2 * PH):
        stream[PQ + m] = k_major(a["w_peer_q"][0][:, m * P:(m + 1) * P])
    stream[EU:EV] = a["expert_u"][0].reshape(NK, NK, KC, P).transpose(0, 3, 2, 1).reshape(NK, P, D)
    stream[EV:GA] = a["expert_v"][0].reshape(NK, NK, D)
    stream[GA:END] = a["w_pl_gate"][0].reshape(KC, P, D)

    cols = np.zeros((P, C_END), np.float32)
    for c0, n in ((C_LNMIX, "ln_mix"), (C_LNFFN, "ln_ffn"), (C_LNPL, "ln_pl")):
        cols[:, c0:c0 + KC] = a[n][0].reshape(KC, P).T
    cols[:, C_YG:C_YG + CC] = a["attn_out_norm"][0].reshape(CC, P).T
    cols[:, C_YG + CC:C_YG + KC] = a["conv_out_norm"][0].reshape(CC, P).T
    cols[:, C_QN] = np.concatenate([a["q_norm"][0]] * 2)
    cols[:, C_KN] = np.concatenate([a["k_norm"][0]] * 2)
    cols[:H, C_BF] = a["b_fgate"][0]
    cols[:, C_CB:C_CB + CC] = a["conv_b"][0].reshape(CC, P).T
    cols[:, C_CW:] = a["conv_w"][0][:, 0].reshape(CW, CC, P).transpose(2, 1, 0).reshape(P, CC * CW)
    rows = np.stack([a["conv_ln_g"][0], a["conv_ln_b"][0]])
    arrays = {
        "x_in": a["x"][0],
        "p_in": a["p"][0, 0].T.reshape(PLE // P, P, S).transpose(1, 0, 2),
        "stream_in": stream,
        "cols_in": cols,
        "rows_in": np.broadcast_to(rows, (P, 2, DA)),
        "keys_in": np.stack([a["sub_keys1"][0].T, a["sub_keys2"][0].T], 1),
    }
    arrays = {k: np.ascontiguousarray(v) for k, v in arrays.items()}
    nc = bacc.Bacc("TRN2", target_bir_lowering=False, num_devices=1)
    aps = [nc.dram_tensor(k, v.shape, F32, kind="ExternalInput").ap() for k, v in arrays.items()]
    out = nc.dram_tensor("layer_out", (S, D), F32, kind="ExternalOutput").ap()
    act_dram = nc.dram_tensor("act_dram", (NK, P, S), F32, kind="Internal").ap()
    gate_dram = nc.dram_tensor("gate_dram", (S // CHUNK, P, NK * CHUNK), F32, kind="Internal").ap()
    hybrid_layer(nc, *aps, out, act_dram, gate_dram)
    r = run(nc, [arrays], core_ids=[0])
    return np.asarray(r.results[0]["layer_out"]).reshape(1, S, D)
```

```python
from contextlib import ExitStack

import concourse.bass as bass
from concourse import mybir
from concourse.alu_op_type import AluOpType as ALU

F32, F32R, BF16, U32 = mybir.dt.float32, mybir.dt.float32r, mybir.dt.bfloat16, mybir.dt.uint32
ACT = mybir.ActivationFunctionType
AX = mybir.AxisListType

P = 128
D = 1024
S = 512
TT = S // P
KC = D // P
DA = 512
CC = DA // P
H = 8
DH = DA // H
CW = 31
PH = 8
TOP = 16
NK = 128
PLE = 256
EPS, LN_EPS = 1e-6, 1e-5
NEG = -1e38

PROJ = 0
GLU = PROJ + PLE // P
FG = GLU + 2 * CC
QK = FG + 1
VV = QK + 2 * CC
WO = VV + CC
PQ = WO + KC
EU = PQ + 2 * PH
EV = EU + NK
GA = EV + NK
END = GA + KC
RING = 4
LEAD = 3
STEP = 16
LAST = 3
CLEAD = 3
CHUNK = 32
GT = 4
GW = GT * CHUNK
UT = 4
UNITS = P // UT
UCHUNK = CHUNK // UT
URING = 4

C_LNMIX, C_LNFFN, C_LNPL, C_YG = 0, KC, 2 * KC, 3 * KC
C_QN = 4 * KC
C_KN = C_QN + 1
C_BF = C_KN + 1
C_CB = C_BF + 1
C_CW = C_CB + CC
C_END = C_CW + CC * CW
N_CONSTS = 26


def slot(s):
    return s % RING


def hybrid_layer(nc, x, pT, stream, cols, rows, keysT, out, act_dram, gate_dram):
    ctx = ExitStack()
    with ctx:
        def sb(name, shape, dt=F32):
            return ctx.enter_context(nc.sbuf_tensor(name, shape, dt))

        def sem(name):
            return ctx.enter_context(nc.semaphore(name))

        xs = sb("xs", [P, TT, D])
        pp = sb("pp", [P, TT, D])
        raw = sb("raw", [P, RING, D])
        whi = sb("whi", [P, RING, D], F32R)
        wlo = sb("wlo", [P, RING, D], F32R)
        ahi = sb("ahi", [P, KC, S], F32R)
        alo = sb("alo", [P, KC, S], F32R)
        colc = sb("colc", [P, C_END])
        ident = sb("ident", [P, P])
        iota = sb("iota", [P, P])
        epsc = sb("epsc", [P, 2])
        qgain = sb("qgain", [P, 1])
        ss = sb("ss", [P, 4, TT, 2])
        ms = sb("ms", [P, 4, TT, 2])
        sd = sb("sd", [P, 4, TT, 2])
        rs = sb("rs", [P, 4, TT, 2])
        diag = sb("diag", [P, TT, 2, P])
        warm = sb("warm", [P, 1])
        junk = sb("junk", [P, D])
        ps = ctx.enter_context(nc.psum_tensor("ps", [P, 8, S], F32))

        front = ctx.enter_context(ExitStack())

        def fb(name, shape, dt=F32):
            return front.enter_context(nc.sbuf_tensor(name, shape, dt))

        lnrows = fb("lnrows", [P, 2, DA])
        negmask = fb("negmask", [P, P], BF16)
        identb = fb("identb", [P, P], BF16)
        blk = fb("blk", [P, 2 * CC, 2 * H])
        self_ = fb("self_", [P, H, P], BF16)
        selq = fb("selq", [P, 2 * CC, P], BF16)
        glu_flat = fb("glu_flat", [P, CC * (CW - 1 + S)])
        glu = glu_flat[:].rearrange("p (c n) -> p c n", c=CC)
        yc = glu_flat[:, 0:TT * DA].rearrange("p (t n) -> p t n", t=TT)
        cy = fb("cy", [P, CC, S])
        vt = fb("vt", [P, TT, DA + DH])
        f3 = fb("f3", [P, S], BF16)
        r3 = fb("r3", [P, S], BF16)
        nmax = fb("nmax", [P, TT * H])
        den = fb("den", [P, TT * H])
        rden = fb("rden", [P, TT * H])
        bn = fb("bn", [P, TT, 6])
        mv = fb("mv", [P, TT, 2])
        lsd = fb("lsd", [P, TT])
        lrs = fb("lrs", [P, TT])
        with ExitStack() as only_projection:
            def ob(name, shape, dt=F32):
                return only_projection.enter_context(nc.sbuf_tensor(name, shape, dt))

            p_raw = ob("p_raw", [P, PLE // P, S])
            p_hi = ob("p_hi", [P, PLE // P, S], F32R)
            p_lo = ob("p_lo", [P, PLE // P, S], F32R)
        qk = fb("qk", [P, 2 * CC, S])
        with ExitStack() as before_attention:
            def ob(name, shape, dt=F32):
                return before_attention.enter_context(nc.sbuf_tensor(name, shape, dt))

            sig = ob("sig", [P, 2, S])
            sq = ob("sq", [P, 2, S])
            rt = ob("rt", [2 * H, S])
            rr = ob("rr", [2 * H, 2, S])
            fz = ob("fz", [H, 4, S])
            negf = ob("negf", [H, 2, S])
            mid = ob("mid", [2 * H, S], BF16)
        vT = sig
        pr = fb("pr", [P, 3, S])
        pT_sb = fb("pT_sb", [P, 2, S])
        att = fb("att", [P, TT, DA])
        csg = fb("csg", [P, 2, DA])
        front.close()

        peer = ctx.enter_context(ExitStack())

        def eb(name, shape, dt=F32):
            return peer.enter_context(nc.sbuf_tensor(name, shape, dt))

        kT = eb("kT", [P, 2, NK])
        qp = eb("qp", [P, 2, S])
        hout = eb("hout", [P, RING, S])
        egb = eb("egb", [P, TT, 3, P])
        egs = eb("egs", [P, 3, P])
        egk = eb("egk", [P, 3, P])
        route = ctx.enter_context(ExitStack())

        def rb(name, shape, dt=F32):
            return route.enter_context(nc.sbuf_tensor(name, shape, dt))

        sc = rb("sc", [P, TT, 2 * PH * NK])
        st = rb("st", [P, 2 * PH, NK])
        st2 = rb("st2", [P, 2, NK])
        v16 = rb("v16", [P, PH, 2, TOP])
        i16 = rb("i16", [P, PH, 2, TOP], U32)
        i16f = rb("i16f", [P, PH, 2, TOP])
        cand = rb("cand", [P, PH // 2, TOP, TOP])
        cand2 = rb("cand2", [P, TOP * TOP])
        vs = rb("vs", [P, PH, TOP])
        ic = rb("ic", [P, PH, TOP], U32)
        ab = rb("ab", [P, 2, PH, TOP], U32)
        abf = rb("abf", [P, 2, PH, TOP])
        eq = rb("eq", [P, PH // 2, TOP, TOP])
        vd = rb("vd", [P, PH, TOP])
        vsum = rb("vsum", [P, PH])
        vrec = rb("vrec", [P, PH])
        route.close()
        gates = ctx.enter_context(ExitStack())

        def rb(name, shape, dt=F32):
            return gates.enter_context(nc.sbuf_tensor(name, shape, dt))

        egT = rb("egT", [P, 3, P])
        key_t = rb("key_t", [P, 2, P], BF16)
        gate_t = rb("gate_t", [P, 3, P], BF16)
        gleft = rb("gleft", [P, P])
        iota4 = rb("iota4", [P, NK, UT], BF16)
        eq1 = rb("eq1", [P, 2, NK, UT], BF16)
        oh2 = rb("oh2", [P, URING, NK, UT], BF16)
        oh1 = rb("oh1", [P, URING, 3, NK, UT], BF16)
        gst = rb("gst", [P, 2, NK, CHUNK])
        gates.close()

        hq = sb("hq", [P, 2, GT, S])
        before_gst = 3 * P * 4 + 5 * P * 2 + P * 4 + (3 + 4 * URING) * NK * UT * 2
        sb("gap", [P, (before_gst - 2 * GT * S * 4) // 4])
        gq = sb("gq", [P, 2, S // CHUNK, GW])
        chi = sb("chi", [P, 4, S], F32R)
        clo = sb("clo", [P, 4, S], F32R)
        cf = qp
        sg = cf
        ov = hout

        p_in = [sem(f"p_in{i}") for i in range(PLE // P)]
        col_in, row_in, key_in = (sem(n) for n in ("col_in", "row_in", "key_in"))
        x_in = [sem(f"x_in{t}") for t in range(TT)]
        w_in = [sem(f"w_in{i}") for i in range(RING)]
        consts = sem("consts")
        qgain_done = sem("qgain_done")
        hi_done, lo_done = sem("hi_done"), sem("lo_done")
        mm_done = sem("mm_done")
        rows_done = sem("rows_done")
        p_hi_done, p_lo_done = sem("p_hi_done"), sem("p_lo_done")
        pp_act, pp_dve = sem("pp_act"), sem("pp_dve")
        NORMS = ("x", "y", "h1", "h2")
        sq_done = {n: sem("sq_" + n) for n in NORMS}
        ms_done = {n: sem("ms_" + n) for n in NORMS}
        sd_done = {n: sem("sd_" + n) for n in NORMS}
        rs_done = {n: sem("rs_" + n) for n in NORMS}
        diag_done = {n: sem("diag_" + n) for n in NORMS}
        tr_done = {n: sem("tr_" + n) for n in NORMS}
        nhi_done = {n: sem("nhi_" + n) for n in NORMS}
        nlo_done = {n: sem("nlo_" + n) for n in NORMS}
        sig_done, glu_done, conv_done = sem("sig_done"), sem("glu_done"), sem("conv_done")
        f_act, negf_done, f3_done = sem("f_act"), sem("negf_done"), sem("f3_done")
        sqk_done, qkraw_done, qk_sum, rt_done, rr_done, r3_done, qk_rms, qk_done = (
            sem(n) for n in ("sqk_done", "qkraw_done", "qk_sum", "rt_done", "rr_done", "r3_done", "qk_rms",
                             "qk_done"))
        vT_done, v_tr, vt_done = sem("vT_done"), sem("v_tr"), sem("vt_done")
        logits, max_done, exp_done, pT_tr, pT_done, o_done, rden_done, att_done = (
            sem(n) for n in ("logits", "max_done", "exp_done", "pT_tr", "pT_done", "o_done", "rden_done",
                             "att_done"))
        cy_tr, ln_stat, ln_mean, ln_sub, lsd_done, lrs_done, ln_gain, ln_out, csg_done, yc_done = (
            sem(n) for n in ("cy_tr", "ln_stat", "ln_mean", "ln_sub", "lsd_done", "lrs_done", "ln_gain", "ln_out",
                             "csg_done", "yc_done"))
        h1_done, h2_done = sem("h1_done"), sem("h2_done")
        u_free = sem("u_free")
        sc_mm, sc_done = sem("sc_mm"), sem("sc_done")
        h_stored = [sem(f"h_stored{i}") for i in range(RING)]
        st_done, st_used, rt_a, vd_done, vexp_done, egb_done = (
            sem(n) for n in ("st_done", "st_used", "routing_steps", "vd_done", "vexp_done", "egb_done"))
        egs_done, eg_tr, egT_done, parts_done = (
            sem(n) for n in ("egs_done", "eg_tr", "egT_done", "parts_done"))
        iota4_done, eq1_done = sem("iota4_done"), sem("eq1_done")
        oh_done, g_mm, g_out = (sem(n) for n in ("oh_done", "g_mm", "g_out"))
        g_stored = [sem("g_stored0"), sem("g_stored1")]
        hq_in, gq_in = [sem("hq_in0"), sem("hq_in1")], [sem("gq_in0"), sem("gq_in1")]
        cf_done, chi_done, clo_done = sem("cf_done"), sem("chi_done"), sem("clo_done")
        sg_done, sgp_pre, ov_done = sem("sg_done"), sem("sgp_pre"), sem("ov_done")
        out_done = [sem(f"out_done{i}") for i in range(4)]

        def wait(e, sm, value, g=None, per=STEP):
            e.wait_ge(sm, value if g is None else g * per + value)

        def turn(n, g, per=STEP):
            return n if g is None else g * per + n

        def split_hi(act, s, g=None):
            if s >= END:
                return
            wait(act, w_in[slot(s)], 16 * (s // RING + 1), g, 16 * STEP // RING)
            if s >= RING:
                wait(act, mm_done, s - RING + 1, g)
            act.activation(whi[:, slot(s)], raw[:, slot(s)], ACT.Copy).then_inc(hi_done, 1)

        def split_lo(dve, s, g=None):
            if s >= END:
                return
            wait(dve, hi_done, s + 1, g)
            dve.tensor_tensor(wlo[:, slot(s)], raw[:, slot(s)], whi[:, slot(s)], ALU.subtract).then_inc(lo_done, 1)

        def u_tile(pe, s, bank, g=None, after=None):
            wait(pe, lo_done, s + 1, g)
            wh = whi[:, slot(s)].rearrange("p (k c) -> p k c", k=KC)
            wl = wlo[:, slot(s)].rearrange("p (k c) -> p k c", k=KC)
            halves = 2 if after else 1
            for i in range(halves):
                tok = slice(i * S // halves, (i + 1) * S // halves)
                if after:
                    pe.wait_ge(nlo_done[after], 4 * (i + 1))
                for k in range(KC):
                    pe.matmul(ps[:, bank, tok], wl[:, k], ahi[:, k, tok], start=(k == 0), stop=False)
                    pe.matmul(ps[:, bank, tok], wh[:, k], alo[:, k, tok], start=False, stop=False)
                    last = pe.matmul(ps[:, bank, tok], wh[:, k], ahi[:, k, tok], start=False, stop=(k == KC - 1))
            last.then_inc(mm_done, 1)

        def v_rows(pe, s, a_hi, a_lo, t, first, final):
            tok = slice(t * P, (t + 1) * P)
            for n, (a, w) in enumerate(((a_lo, whi), (a_hi, wlo), (a_hi, whi))):
                for half in range(2):
                    last = pe.matmul(ps[:, 2 * t + half], a[:, tok], w[:, slot(s), half * S:(half + 1) * S],
                                     start=(first and n == 0), stop=(final and n == 2))
            return last

        def v_tile(pe, s, a_hi, a_lo, first, g=None, after=None):
            wait(pe, lo_done, s + 1, g)
            for t in ((1, 2, 3, 0) if s == EV and first else range(TT)):
                if after and t % 2 == 0:
                    pe.wait_ge(nlo_done[after], 2 * t + 4)
                if s == EV and first and t == 0:
                    pe.wait_ge(u_free, 2 * PH + NK)
                last = v_rows(pe, s, a_hi, a_lo, t, first, False)
            last.then_inc(mm_done, 1)

        def v_last(pe, end, parts, ready=None, first=False, then_norm=None):
            tiles = range(end - (2 if first else LAST), end)
            for t in range(TT):
                for s in tiles:
                    if t == 0:
                        pe.wait_ge(lo_done, s + 1)
                        if ready:
                            ready(s)
                    last = v_rows(pe, s, *parts(s), t, first and s == tiles[0], s == end - 1)
                    if t == TT - 1:
                        last.then_inc(mm_done, 1)
                    elif s == end - 1:
                        last.then_inc(rows_done, 1)
                if t == TT - 2 and then_norm:
                    norm_pe(pe, then_norm, 0)

        def deferred(s):
            return s in (PQ + 1, PQ + 2, GA + 1, GA + 2)

        def wait_rows(e, s, t):
            if t < TT - 1:
                e.wait_ge(rows_done, (TT - 1) * (GLU - 1, PQ - 1, GA - 1, END - 1).index(s) + t + 1)
            else:
                e.wait_ge(mm_done, s + 1)

        def norm_src(name, t, g):
            if name == "y":
                return (att, yc)[g][:, t]
            return xs[:, t]

        def groups(name):
            return 2 if name == "y" else 1

        def width(name):
            return D // groups(name)

        squares = {n: 0 for n in NORMS}

        def norm_act_squares(act, name, t, gs=None):
            n = NORMS.index(name)
            for g in range(groups(name)) if gs is None else gs:
                half = squares[name] % groups(name)
                if squares[name] >= groups(name):
                    act.wait_ge(sq_done[name], squares[name] - groups(name) + 1)
                squares[name] += 1
                act.activation(junk[:, half * width(name):(half + 1) * width(name)], norm_src(name, t, g),
                               ACT.Square, accum_out=ss[:, n, t, g:g + 1]).then_inc(sq_done[name], 1)

        def norm_act_root(act, name, t):
            n, G = NORMS.index(name), groups(name)
            act.wait_ge(ms_done[name], t + 1)
            act.activation(sd[:, n, t, :G], ms[:, n, t, :G], ACT.Sqrt).then_inc(sd_done[name], 1)

        def norm_dve_mean(dve, name, t):
            n, G = NORMS.index(name), groups(name)
            dve.wait_ge(sq_done[name], G * (TT if name == "y" else t + 1))
            dve.tensor_scalar(ms[:, n, t, :G], ss[:, n, t, :G], 1.0 / width(name), EPS, ALU.mult,
                              ALU.add).then_inc(ms_done[name], 1)

        def norm_dve_diag(dve, name, t):
            n, G = NORMS.index(name), groups(name)
            dve.wait_ge(sd_done[name], t + 1)
            dve.reciprocal(rs[:, n, t, :G], sd[:, n, t, :G]).then_inc(rs_done[name], 1)
            dve.wait_ge(rs_done[name], t + 1)
            for g in range(G):
                dve.tensor_scalar(diag[:, t, g], ident[:], rs[:, n, t, g:g + 1], None,
                                  ALU.mult).then_inc(diag_done[name], 1)

        def norm_pe(pe, name, pair):
            G = groups(name)
            if name in ("h1", "h2"):
                pe.wait_ge(h1_done if name == "h1" else h2_done, 2 * pair + 2)
            for i in range(2):
                t = 2 * pair + i
                pe.wait_ge(diag_done[name], G * (t + 1))
                for b in range(4):
                    for c in range(2):
                        k = 2 * b + c
                        g, col = (k // 4, k % 4) if G == 2 else (0, k)
                        last = pe.matmul(ps[:, 4 * pair + b, (2 * c + i) * P:(2 * c + i + 1) * P],
                                         norm_src(name, t, g)[:, col * P:(col + 1) * P], diag[:, t, g],
                                         start=True, stop=True)
                    if i == 1:
                        last.then_inc(tr_done[name], 1)

        GAIN = {"x": C_LNMIX, "y": C_YG, "h1": C_LNFFN, "h2": C_LNPL}

        def norm_dst(buf, t, b):
            return buf[:, 4 * b:4 * b + 4, t * P:(t + 1) * P]

        def norm_part(n, c):
            pair, b = n // 4, n % 4
            return 2 * b + c, slice(2 * c * P, 2 * (c + 1) * P), slice(2 * pair * P, 2 * (pair + 1) * P)

        def norm_act_hi(act, name, n):
            act.wait_ge(tr_done[name], n + 1)
            for c in range(2):
                k, part, tok = norm_part(n, c)
                last = act.activation(ahi[:, k, tok], ps[:, n, part], ACT.Copy,
                                      scale=colc[:, GAIN[name] + k:GAIN[name] + k + 1])
            last.then_inc(nhi_done[name], 1)

        def norm_dve_lo(dve, name, n):
            dve.wait_ge(nhi_done[name], n + 1)
            for c in range(2):
                k, part, tok = norm_part(n, c)
                last = dve.scalar_tensor_tensor(alo[:, k, tok], ps[:, n, part],
                                                colc[:, GAIN[name] + k:GAIN[name] + k + 1], ahi[:, k, tok],
                                                ALU.mult, ALU.subtract)
            last.then_inc(nlo_done[name], 1)

        def norm_act(act, name, ready):
            act.activation(warm[:], epsc[:, 0:1], ACT.Sqrt)
            for t in range(TT):
                act.wait_ge(ready, t + 1)
                norm_act_squares(act, name, t)
                norm_act_root(act, name, t)
                if t >= TT - 2:
                    for n in range(4 * (t - TT + 2), 4 * (t - TT + 3)):
                        norm_act_hi(act, name, n)

        def norm_dve(dve, name, s, ready):
            for t in range(TT):
                wait_rows(dve, s, t)
                dve.tensor_tensor(xs[:, t].rearrange("p (b n) -> p b n", b=2), ps[:, 2 * t:2 * t + 2],
                                  xs[:, t].rearrange("p (b n) -> p b n", b=2), ALU.add).then_inc(ready, 1)
                norm_dve_mean(dve, name, t)
                norm_dve_diag(dve, name, t)
                if t >= TT - 2:
                    for n in range(4 * (t - TT + 2), 4 * (t - TT + 3)):
                        norm_dve_lo(dve, name, n)

        QK_BANKS = (2, 3, 6, 7)
        LN_AT = 20
        HEADS = [(q, h) for q in range(TT) for h in range(H)]

        def units(j):
            return [(j - 4) * 4 + i for i in range(4)] if 4 <= j < 4 + UNITS // 4 else []

        block = ctx.enter_context(nc.Block())

        @block.sync
        def _(sp):
            def load(s, g=None):
                if s >= END:
                    return
                if s >= RING:
                    wait(sp, lo_done, s - RING + 1, g)
                sp.dma_start(raw[:, slot(s)], stream[turn(s, g)]).then_inc(w_in[slot(s)], 16)

            for i in range(PLE // P):
                load(i)
                sp.dma_start(p_raw[:, i], pT[:, i]).then_inc(p_in[i], 16)
            for t in range(TT):
                sp.dma_start(xs[:, t], x[t * P:(t + 1) * P, :]).then_inc(x_in[t], 16)
            sp.dma_start(colc[:], cols).then_inc(col_in, 16)
            sp.dma_start(lnrows[:], rows).then_inc(row_in, 16)
            for s in range(2, EU):
                load(s)
                if s == WO + 3:
                    sp.wait_ge(nlo_done["y"], 2 * TT)
                    sp.dma_start(kT[:], keysT).then_inc(key_in, 16)
            with sp.Fori(0, NK // STEP) as g:
                for j in range(STEP):
                    load(EU + j, g)

            def load_group(n, g=None):
                b = n % 2
                if g is None:
                    h_src, g_src = act_dram[GT * n:GT * n + GT], gate_dram[:, :, n * GW:(n + 1) * GW]
                else:
                    h_src = act_dram[bass.ds(g * STEP + GT * n, GT)]
                    g_src = gate_dram[:, :, bass.ds(g * (STEP * CHUNK) + n * GW, GW)]
                sp.dma_start(hq[:, b], h_src.rearrange("a p t -> p a t")).then_inc(hq_in[b], 16)
                sp.dma_start(gq[:, b], g_src.rearrange("c p n -> p c n")).then_inc(gq_in[b], 16)

            for s in range(EV, EV + RING - 1):
                load(s)
            for i in range(RING):
                sp.wait_ge(h_stored[i], 16 * 2 * GT // RING)
            for b in range(2):
                sp.wait_ge(g_stored[b], 16 * S // CHUNK // 2)
            sp.wait_ge(g_mm, UNITS * TT)
            load_group(0)
            load_group(1)
            load(EV + RING - 1)
            for i in range(RING):
                sp.wait_ge(h_stored[i], 16 * NK // RING)
            with sp.Fori(0, NK // STEP - 1) as g:
                for j in range(STEP):
                    load(EV + RING + j, g)
                    if j % GT == GT - 1:
                        wait(sp, cf_done, j + 1, g)
                        load_group(2 + j // GT, g)
            for s in range(EV + NK - STEP + RING, END):
                load(s)
                m = s - EV - RING
                if m % GT == GT - 1 and m // GT + 2 < NK // GT:
                    sp.wait_ge(cf_done, m + 1)
                    load_group(2 + m // GT)
            for n in range(2 * TT):
                t, half = n // 2, n % 2
                sp.wait_ge(ov_done, n + 1)
                sp.dma_start(out[t * P:(t + 1) * P, half * S:(half + 1) * S], ov[:, n % 4]).then_inc(out_done[n % 4], 16)
            for i in range(4):
                sp.wait_ge(out_done[i], 16 * 2 * TT // 4)

        @block.gpsimd
        def _(pool):
            n = [0]

            def step(ins):
                ins.then_inc(consts, 1)
                n[0] += 1
                if n[0] < N_CONSTS:
                    pool.wait_ge(consts, n[0])

            step(pool.memset(ident[:], 0.0))
            step(pool.affine_select(out=ident[:], in_=ident[:], compare_op=ALU.not_equal, fill=1.0, base=0,
                                    pattern=[[-1, P]], channel_multiplier=1))
            step(pool.memset(epsc[:, 0:1], EPS))
            step(pool.memset(epsc[:, 1:2], LN_EPS))
            step(pool.memset(glu[:, :, 0:CW - 1], 0.0))
            step(pool.memset(blk[:], 0.0))
            for i in range(2):
                step(pool.affine_select(out=blk[i * DH:(i + 1) * DH], in_=blk[i * DH:(i + 1) * DH],
                                        compare_op=ALU.not_equal, fill=1.0, base=-i,
                                        pattern=[[-2, 2 * CC], [1, 2 * H]], channel_multiplier=0))
            step(pool.memset(negmask[:], 0.0))
            step(pool.affine_select(out=negmask[:], in_=negmask[:], compare_op=ALU.is_ge, fill=NEG, base=0,
                                    pattern=[[-1, P]], channel_multiplier=1))
            step(pool.tensor_copy(identb[:], ident[:]))
            step(pool.memset(self_[:], 0.0))
            step(pool.memset(selq[:], 0.0))
            step(pool.memset(f3[:], 0.0))
            step(pool.memset(r3[:], 0.0))
            step(pool.memset(vt[:, :, DA:], 0.0))
            for base in (0, 32, 64):
                step(pool.affine_select(out=self_[base:base + 32], in_=self_[base:base + 32],
                                        compare_op=ALU.not_equal, fill=1.0, base=0,
                                        pattern=[[-1, H], [0, P]], channel_multiplier=1))
                for i in range(2):
                    part = selq[base:base + 32, :, i * DH:(i + 1) * DH]
                    step(pool.affine_select(out=part, in_=part, compare_op=ALU.not_equal, fill=1.0, base=-i,
                                            pattern=[[-2, 2 * CC], [0, DH]], channel_multiplier=1))
            step(pool.iota(iota[:], pattern=[[1, P]], base=0, channel_multiplier=0,
                           allow_small_or_imprecise_dtypes=True))
            assert n[0] == N_CONSTS

        @block.scalar
        def _(act):
            def v_copy(n):
                act.wait_ge(v_tr, n + 1)
                act.activation(vt[:, :, n * P:(n + 1) * P], ps[:, 4 + n % 2].rearrange("p (t c) -> p t c", t=TT),
                               ACT.Copy).then_inc(vt_done, 1)

            for i in range(PLE // P):
                split_hi(act, i)
                act.wait_ge(p_in[i], 16)
                act.activation(p_hi[:, i], p_raw[:, i], ACT.Copy).then_inc(p_hi_done, 1)
            for t in range(TT):
                act.wait_ge(x_in[t], 16)
                norm_act_squares(act, "x", t)
            for t in range(TT):
                norm_act_root(act, "x", t)
            for t in range(TT):
                wait_rows(act, GLU - 1, t)
                act.activation(pp[:, t, 0:S], ps[:, 2 * t], ACT.Copy).then_inc(pp_act, 1)
                if t == 1:
                    split_hi(act, GLU)
            act.wait_ge(col_in, 16)
            for n in range(2 * TT):
                norm_act_hi(act, "x", n)
            for s in range(GLU + 1, GLU + LEAD):
                split_hi(act, s)
            act.wait_ge(consts, N_CONSTS)
            for s in range(GLU, WO):
                split_hi(act, s + LEAD)
                if s < FG:
                    if (s - GLU) % 2 == 0:
                        c = (s - GLU) // 2
                        act.wait_ge(mm_done, s + 1)
                        if c >= 2:
                            act.wait_ge(glu_done, c - 1)
                        act.activation(sig[:, c % 2], ps[:, 0], ACT.Sigmoid).then_inc(sig_done, 1)
                elif s == FG:
                    act.wait_ge(mm_done, s + 1)
                    act.activation(fz[:, 0], ps[0:H, 0], ACT.Identity,
                                   bias=colc[0:H, C_BF:C_BF + 1]).then_inc(f_act, 1)
                    act.wait_ge(f_act, 1)
                    act.activation(fz[:, 1], fz[:, 0], ACT.Abs).then_inc(f_act, 1)
                    act.wait_ge(f_act, 2)
                    act.activation(fz[:, 2], fz[:, 1], ACT.Exp, scale=-1.0).then_inc(f_act, 1)
                    act.wait_ge(f_act, 3)
                    act.activation(fz[:, 3], fz[:, 2], ACT.Ln, bias=1.0).then_inc(f_act, 1)
                elif s < VV:
                    n = s - QK
                    act.wait_ge(mm_done, s + 1)
                    if n >= 2:
                        act.wait_ge(qk_sum, n - 1)
                    act.activation(sq[:, n % 2], ps[:, s % 2], ACT.Square).then_inc(sqk_done, 1)
                    act.activation(qk[:, n], ps[:, s % 2], ACT.Copy).then_inc(qkraw_done, 1)
                else:
                    n = s - VV
                    if n == 0:
                        act.wait_ge(qk_sum, 2 * CC)
                        act.activation(rt[:], ps[0:2 * H, 2], ACT.Sqrt, bias=epsc[0:2 * H, 0:1],
                                       scale=1.0 / DH).then_inc(rt_done, 1)
                    act.wait_ge(mm_done, s + 1)
                    if n >= 2:
                        act.wait_ge(v_tr, n - 1)
                    act.activation(vT[:, n % 2], ps[:, s % 2], ACT.Copy).then_inc(vT_done, 1)
                    if n >= 1:
                        v_copy(n - 1)
            v_copy(CC - 1)
            for i in range(len(HEADS) + 1):
                if i == LN_AT + 5:
                    act.wait_ge(ln_mean, TT)
                    act.activation(lsd[:], mv[:, :, 1], ACT.Sqrt, bias=epsc[:, 1:2]).then_inc(lsd_done, 1)
                if i == LN_AT + 9:
                    for t in range(TT):
                        act.wait_ge(ln_out, t + 1)
                        if t >= 2:
                            act.wait_ge(yc_done, t - 1)
                        act.activation(csg[:, t % 2], yc[:, t], ACT.Sigmoid).then_inc(csg_done, 1)
                if i < len(HEADS):
                    q, h = HEADS[i]
                    n = (q + 1) * P
                    act.wait_ge(max_done, i + 1)
                    if i >= 3:
                        act.wait_ge(pT_tr, i - 2)
                    act.activation(pr[:, i % 3, :n], ps[:, 2 + i % 2, :n], ACT.Exp, bias=nmax[:, i:i + 1],
                                   accum_out=den[:, i:i + 1]).then_inc(exp_done, 1)
                if i >= 1:
                    q, h = HEADS[i - 1]
                    n = (q + 1) * P
                    act.wait_ge(pT_tr, i)
                    if i >= 3:
                        act.wait_ge(o_done, i - 2)
                    act.activation(pT_sb[:, (i - 1) % 2, :n], ps[:, 4 + (i - 1) % 2, :n],
                                   ACT.Copy).then_inc(pT_done, 1)
                if i == len(HEADS) - 2:
                    act.wait_ge(att_done, 2 * (TT - 1))
                    for t in range(TT - 1):
                        norm_act_squares(act, "y", t, [0])
                if i == len(HEADS) - 1:
                    for t in range(TT):
                        act.wait_ge(yc_done, t + 1)
                        norm_act_squares(act, "y", t, [1])
            act.activation(warm[:], epsc[:, 0:1], ACT.Sqrt)
            act.wait_ge(att_done, 2 * TT)
            norm_act_squares(act, "y", TT - 1, [0])
            for t in range(TT):
                norm_act_root(act, "y", t)
            act.wait_ge(mm_done, WO)
            for n in range(2 * TT):
                norm_act_hi(act, "y", n)
            for s in range(WO, WO + KC):
                if not deferred(s + LEAD):
                    split_hi(act, s + LEAD)
            norm_act(act, "h1", h1_done)
            for s in (PQ + 1, PQ + 2):
                split_hi(act, s)
            for s in range(PQ, EU + 1):
                n = s - PQ
                if s < EU:
                    split_hi(act, s + LEAD)
                    act.wait_ge(mm_done, s + 1)
                    if n >= 2:
                        act.wait_ge(sc_mm, n - 1)
                    act.activation(qp[:, n % 2], ps[:, s % 2], ACT.Copy).then_inc(u_free, 1)
                if n >= 1:
                    act.wait_ge(sc_mm, n)
                    act.activation(sc[:, :, (n - 1) * NK:n * NK],
                                   ps[:, 2 + (n - 1) % 2].rearrange("p (t k) -> p t k", t=TT),
                                   ACT.Copy).then_inc(sc_done, 1)

            def gelu(n, g=None):
                wait(act, mm_done, EU + n + 1, g)
                if n >= RING:
                    wait(act, h_stored[n % RING], 16 * (n // RING), g, 16 * STEP // RING)
                act.activation(hout[:, n % RING], ps[:, (EU + n) % 2], ACT.Gelu_apprx_tanh).then_inc(u_free, 1)
                wait(act, u_free, 2 * PH + n + 1, g)
                act.dma_start(act_dram[turn(n, g)], hout[:, n % RING]).then_inc(h_stored[n % RING], 16)

            def routing_turn(it, g=None):
                if it >= 1:
                    wait(act, st_used, it, g, 1)
                act.activation(st[:], sc[:, turn(it, g, 1)].rearrange("p (h k) -> p h k", k=NK),
                               ACT.Copy).then_inc(st_done, 1)
                for j in range(STEP):
                    split_hi(act, EU + it * STEP + j + LEAD, g)
                    gelu(it * STEP + j, g)
                wait(act, vd_done, it + 1, g, 1)
                act.activation(vd[:], vd[:], ACT.Exp).then_inc(vexp_done, 1)

            act.wait_ge(sc_done, 2 * PH)
            routing_turn(0)
            with act.Fori(0, TT - 1) as g:
                routing_turn(1, g)

            def gate_turn(it, g=None):
                for j in range(STEP):
                    if j == 1:
                        wait(act, egb_done, TT)
                        if it >= 1:
                            wait(act, eg_tr, it, g, 1)
                        act.activation(egs[:], egb[:, turn(it, g, 1)], ACT.Copy).then_inc(egs_done, 1)
                    split_hi(act, EU + (TT + it) * STEP + j + LEAD, g)
                    if it == TT - 1 and j == STEP - 1:
                        first_coefs()
                    else:
                        gelu((TT + it) * STEP + j, g)
                    if j == 2:
                        wait(act, eg_tr, it + 1, g, 1)
                        if it >= 1:
                            wait(act, parts_done, 6 * it, g, 6)
                        act.activation(egT[:], ps[:, 6, 0:3 * P].rearrange("p (n t) -> p n t", n=3),
                                       ACT.Copy).then_inc(egT_done, 1)
                    for u in units(j):
                        k = UNITS * it + u
                        buf = (u // UCHUNK) % 2
                        wait(act, g_mm, k + 1, g, UNITS)
                        if u % UCHUNK == 0 and k >= 2 * UCHUNK:
                            wait(act, g_stored[buf], 16 * (k // UCHUNK // 2), g, 16 * P // CHUNK // 2)
                        tok = (u % UCHUNK) * UT
                        act.activation(gst[:, buf, :, tok:tok + UT].rearrange("p e t -> p t e"),
                                       ps[:, 2 + u % 4].rearrange("p (t e) -> p t e", t=UT),
                                       ACT.Copy).then_inc(g_out, 1)
                        if u % UCHUNK == UCHUNK - 1:
                            wait(act, g_out, k + 1, g, UNITS)
                            act.dma_start(gate_dram[turn(k // UCHUNK, g, P // CHUNK)],
                                          gst[:, buf].rearrange("p e t -> p (e t)")).then_inc(g_stored[buf], 16)

            def coef_hi(m, g=None):
                if m >= NK:
                    return
                wait(act, cf_done, m + 1, g)
                if m >= 4:
                    wait(act, mm_done, EV + m - 3, g)
                act.activation(chi[:, m % 4], cf[:, m % 2], ACT.Copy).then_inc(chi_done, 1)

            def expert_v_turn(it, g=None):
                for j in range(STEP):
                    if g is not None or not deferred(EV + it * STEP + j + LEAD):
                        split_hi(act, EV + it * STEP + j + LEAD, g)
                    coef_hi(it * STEP + j + CLEAD, g)

            def first_coefs():
                for b in range(2):
                    act.wait_ge(g_stored[b], 16 * S // CHUNK // 2)
                for m in range(CLEAD):
                    coef_hi(m)
                    if m == 0:
                        gelu(NK - 1)

            gate_turn(0)
            with act.Fori(0, TT - 2) as g:
                gate_turn(1, g)
            gate_turn(TT - 1)
            expert_v_turn(0)
            with act.Fori(0, NK // STEP - 2) as g:
                expert_v_turn(1, g)
            expert_v_turn(NK // STEP - 1)
            norm_act(act, "h2", h2_done)
            for s in (GA + 1, GA + 2):
                split_hi(act, s)
            act.activation(warm[:], epsc[:, 0:1], ACT.Sigmoid)
            for s in range(GA, END):
                split_hi(act, s + LEAD)
            for n in range(2 * TT):
                wait_rows(act, END - 1, n // 2)
                if n >= 2:
                    act.wait_ge(ov_done, n - 1)
                act.activation(sg[:, n % 2], ps[:, n], ACT.Sigmoid).then_inc(sg_done, 1)

        @block.vector
        def _(dve):
            for i in range(PLE // P):
                split_lo(dve, i)
                dve.wait_ge(p_hi_done, i + 1)
                dve.tensor_tensor(p_lo[:, i], p_raw[:, i], p_hi[:, i], ALU.subtract).then_inc(p_lo_done, 1)
            for t in range(TT):
                norm_dve_mean(dve, "x", t)
            dve.wait_ge(consts, N_CONSTS)
            for t in range(TT):
                if t == 2:
                    for u in range(TT):
                        norm_dve_diag(dve, "x", u)
                wait_rows(dve, GLU - 1, t)
                dve.tensor_copy(pp[:, t, S:], ps[:, 2 * t + 1]).then_inc(pp_dve, 1)
            split_lo(dve, GLU)
            dve.wait_ge(col_in, 16)
            dve.tensor_scalar(qgain[:], colc[:, C_QN:C_QN + 1], DH ** -0.5, None, ALU.mult).then_inc(qgain_done, 1)
            for n in range(2 * TT):
                norm_dve_lo(dve, "x", n)
            for s in range(GLU + 1, GLU + LEAD):
                split_lo(dve, s)

            conv = [0]

            def conv_taps(count, channels):
                for _ in range(count):
                    n = conv[0]
                    if n >= channels * CW:
                        return
                    conv[0] += 1
                    c, w = n // CW, n % CW
                    src = glu[:, c, w:w + S]
                    tap = colc[:, C_CW + c * CW + w:C_CW + c * CW + w + 1]
                    if w == 0:
                        dve.wait_ge(glu_done, c + 1)
                        dve.tensor_scalar(cy[:, c], src, tap, colc[:, C_CB + c:C_CB + c + 1], ALU.mult,
                                          ALU.add).then_inc(conv_done, 1)
                    else:
                        dve.wait_ge(conv_done, n)
                        dve.scalar_tensor_tensor(cy[:, c], src, tap, cy[:, c], ALU.mult,
                                                 ALU.add).then_inc(conv_done, 1)

            def three_parts(dst, a, rows_n, left, done):
                dve.tensor_copy(dst[0:rows_n], a).then_inc(done, 1)
                dve.wait_ge(done, 1)
                dve.tensor_tensor(left, a, dst[0:rows_n], ALU.subtract).then_inc(done, 1)
                dve.wait_ge(done, 2)
                dve.tensor_copy(mid[0:rows_n], left).then_inc(done, 1)
                dve.wait_ge(done, 3)
                dve.tensor_copy(dst[32:32 + rows_n], mid[0:rows_n]).then_inc(done, 1)
                dve.tensor_tensor(left, left, mid[0:rows_n], ALU.subtract).then_inc(done, 1)
                dve.wait_ge(done, 5)
                dve.tensor_copy(dst[64:64 + rows_n], left).then_inc(done, 1)

            def qk_norm(n):
                dve.wait_ge(qk_rms, n + 1)
                dve.wait_ge(qgain_done, 1)
                gain = colc[:, C_KN:C_KN + 1] if n % 2 else qgain[:]
                dve.scalar_tensor_tensor(qk[:, n], qk[:, n], gain, ps[:, QK_BANKS[n % 4]], ALU.mult,
                                         ALU.mult).then_inc(qk_done, 1)

            for s in range(GLU, WO):
                split_lo(dve, s + LEAD)
                if s < FG and (s - GLU) % 2 == 1:
                    c = (s - GLU) // 2
                    dve.wait_ge(mm_done, s + 1)
                    dve.wait_ge(sig_done, c + 1)
                    dve.tensor_tensor(glu[:, c, CW - 1:], ps[:, 1], sig[:, c % 2], ALU.mult).then_inc(glu_done, 1)
                if s == FG + 1:
                    dve.wait_ge(f_act, 4)
                    dve.scalar_tensor_tensor(fz[:, 1], fz[:, 0], 0.0, fz[:, 3], ALU.min,
                                             ALU.subtract).then_inc(negf_done, 1)
                    dve.wait_ge(negf_done, 1)
                    dve.tensor_scalar(fz[:, 2], fz[:, 1], -1.0, None, ALU.mult).then_inc(negf_done, 1)
                    dve.wait_ge(negf_done, 2)
                    dve.tensor_tensor_scan(negf[:, 0], fz[:, 2], fz[:, 2], 0.0, ALU.add,
                                           ALU.bypass).then_inc(negf_done, 1)
                    dve.wait_ge(negf_done, 3)
                    three_parts(f3, negf[:, 0], H, negf[:, 1], f3_done)
                if s == VV + 1:
                    dve.wait_ge(rt_done, 1)
                    dve.reciprocal(rr[:, 0], rt[:]).then_inc(rr_done, 1)
                    dve.wait_ge(rr_done, 1)
                    three_parts(r3, rr[:, 0], 2 * H, rr[:, 1], r3_done)
                if s > GLU + 1:
                    conv_taps(5 if s < VV else 2, max(0, min(CC, (s - GLU) // 2)))
            for n in range(2 * CC):
                qk_norm(n)

            def heads_out(q, b):
                k, hs = 2 * q + b, slice(q * H + 4 * b, q * H + 4 * b + 4)
                dve.wait_ge(exp_done, hs.stop)
                dve.reciprocal(rden[:, hs], den[:, hs]).then_inc(rden_done, 1)
                dve.wait_ge(rden_done, k + 1)
                dve.wait_ge(o_done, hs.stop)
                dve.tensor_tensor(att[:, q, 4 * b * DH:4 * (b + 1) * DH].rearrange("p (h d) -> p h d", h=4),
                                  ps[:, 6 + b, 0:4 * DH].rearrange("p (h d) -> p h d", h=4),
                                  rden[:, hs].unsqueeze(2).broadcast_to([P, 4, DH]),
                                  ALU.mult).then_inc(att_done, 1)

            def ln_center(t):
                dve.wait_ge(cy_tr, t + 1)
                dve.bn_stats(bn[:, t], ps[:, t % 2]).then_inc(ln_stat, 1)
                dve.wait_ge(ln_stat, t + 1)
                dve.bn_aggr(mv[:, t], bn[:, t]).then_inc(ln_mean, 1)
                dve.wait_ge(ln_mean, t + 1)
                dve.tensor_scalar(yc[:, t], ps[:, t % 2], mv[:, t, 0:1], None, ALU.subtract).then_inc(ln_sub, 1)

            def ln_scale(t):
                if t == 0:
                    dve.wait_ge(lsd_done, 1)
                    dve.reciprocal(lrs[:], lsd[:]).then_inc(lrs_done, 1)
                    dve.wait_ge(lrs_done, 1)
                    dve.wait_ge(row_in, 16)
                dve.scalar_tensor_tensor(yc[:, t], yc[:, t], lrs[:, t:t + 1], lnrows[:, 0], ALU.mult,
                                         ALU.mult).then_inc(ln_gain, 1)
                dve.wait_ge(ln_gain, t + 1)
                dve.tensor_tensor(yc[:, t], yc[:, t], lnrows[:, 1], ALU.add).then_inc(ln_out, 1)

            def swish(t):
                dve.wait_ge(csg_done, t + 1)
                dve.tensor_tensor(yc[:, t], yc[:, t], csg[:, t % 2], ALU.mult).then_inc(yc_done, 1)

            for i in range(len(HEADS) + 2):
                if i < len(HEADS):
                    q, h = HEADS[i]
                    n = (q + 1) * P
                    dve.wait_ge(logits, i + 1)
                    dve.tensor_reduce(nmax[:, i:i + 1], ps[:, 2 + i % 2, :n], AX.X, ALU.max,
                                      negate=True).then_inc(max_done, 1)
                if i >= 2 and (i - 2) % 4 == 3:
                    heads_out((i - 2) // H, (i - 2) // 4 % 2)
                if i < LN_AT:
                    conv_taps(CC * CW if i == LN_AT - 1 else 2, CC)
                elif i < LN_AT + TT:
                    ln_center(i - LN_AT)
                elif LN_AT + 5 <= i < LN_AT + 5 + TT:
                    ln_scale(i - LN_AT - 5)
                elif i in (LN_AT + 9, LN_AT + 10):
                    for t in (0, 1) if i == LN_AT + 9 else (2, 3):
                        swish(t)
            for t in range(TT):
                norm_dve_mean(dve, "y", t)
            for t in range(TT):
                norm_dve_diag(dve, "y", t)
            for n in range(2 * TT):
                norm_dve_lo(dve, "y", n)
            for s in range(WO, WO + KC):
                if not deferred(s + LEAD):
                    split_lo(dve, s + LEAD)
            norm_dve(dve, "h1", PQ - 1, h1_done)
            for s in (PQ + 1, PQ + 2):
                split_lo(dve, s)
            for s in range(PQ, EU):
                split_lo(dve, s + LEAD)
            dve.wait_ge(sc_done, 2 * PH)

            def routing_turn(it, g=None):
                n = [0]

                def step(ins):
                    n[0] += 1
                    ins.then_inc(rt_a, 1)
                    return n[0]

                def need(k):
                    dve.wait_ge(rt_a, k)

                def top16(top_at, idx_at, src, rest):
                    k = [step(dve.max(top_at(r)[:, 0:8], src(r))) for r in range(len(rest))]
                    need(k[-1])
                    k = [step(dve.match_replace(rest[r], top_at(r)[:, 0:8], src(r), NEG)) for r in range(len(rest))]
                    for r in range(len(rest)):
                        step(dve.max_index(idx_at(r)[:, 0:8], top_at(r)[:, 0:8], src(r)))
                    need(k[-1])
                    k = [step(dve.max(top_at(r)[:, 8:16], rest[r])) for r in range(len(rest))]
                    need(k[-1])
                    for r in range(len(rest)):
                        last = step(dve.max_index(idx_at(r)[:, 8:16], top_at(r)[:, 8:16], rest[r]))
                    return last

                def candidates(h0):
                    shape = [P, PH // 2, TOP, TOP]
                    return step(dve.tensor_tensor(
                        cand[:], v16[:, h0:h0 + 4, 0].unsqueeze(3).broadcast_to(shape),
                        v16[:, h0:h0 + 4, 1].unsqueeze(2).broadcast_to(shape), ALU.add))

                def resolve(h0):
                    hs = slice(h0, h0 + 4)
                    shape = [P, PH // 2, TOP, TOP]
                    step(dve.tensor_scalar(ab[:, 0, hs], ic[:, hs], 4, None, ALU.logical_shift_right))
                    k = step(dve.tensor_scalar(ab[:, 1, hs], ic[:, hs], 15, None, ALU.bitwise_and))
                    need(k)
                    k = step(dve.tensor_copy(abf[:, :, hs], ab[:, :, hs]))
                    for half in range(2):
                        need(k)
                        k = step(dve.tensor_tensor(
                            eq[:], abf[:, half, hs].unsqueeze(3).broadcast_to(shape),
                            iota[:, 0:TOP].unsqueeze(1).unsqueeze(1).broadcast_to(shape), ALU.is_equal))
                        need(k)
                        k = step(dve.tensor_tensor(
                            eq[:], eq[:], i16f[:, hs, half].unsqueeze(2).broadcast_to(shape), ALU.mult))
                        need(k)
                        k = step(dve.tensor_reduce(
                            egk[:, half, h0 * TOP:(h0 + 4) * TOP].rearrange("p (h j) -> p h j", h=4), eq[:],
                            AX.X, ALU.add))
                    return k

                wait(dve, st_done, it + 1, g, 1)
                if it >= 1:
                    wait(dve, egb_done, it, g, 1)
                for j in range(STEP):
                    split_lo(dve, EU + it * STEP + j + LEAD, g)
                    if j < PH:
                        last = top16(lambda r: v16[:, j, r], lambda r: i16[:, j, r], lambda r: st[:, 2 * j + r],
                                     [st2[:, 0], st2[:, 1]])
                        if j == PH - 1:
                            need(last)
                            dve.tensor_copy(i16f[:], i16[:]).then_inc(st_used, 1)
                    else:
                        h = j - PH
                        if h == 0:
                            wait(dve, st_used, it + 1, g, 1)
                        if h % 4 == 0:
                            need(candidates(h))
                        last = top16(lambda r: vs[:, h], lambda r: ic[:, h],
                                     lambda r: cand[:, h % 4].rearrange("p a b -> p (a b)"), [cand2[:]])
                        if h == PH - 1:
                            need(last)
                            dve.tensor_tensor(vd[:], vs[:], vs[:, :, 0:1].broadcast_to([P, PH, TOP]),
                                              ALU.subtract).then_inc(vd_done, 1)
                        if h % 4 == 3:
                            need(last)
                            last = resolve(h - 3)
                wait(dve, vexp_done, it + 1, g, 1)
                k = step(dve.tensor_reduce(vsum[:], vd[:], AX.X, ALU.add))
                need(k)
                k = step(dve.reciprocal(vrec[:], vsum[:]))
                need(k)
                k = step(dve.tensor_tensor(egk[:, 2].rearrange("p (h j) -> p h j", h=PH), vd[:],
                                           vrec[:].unsqueeze(2).broadcast_to([P, PH, TOP]), ALU.mult))
                need(k)
                dve.sem_clear(rt_a)
                dve.tensor_copy(egb[:, turn(it, g, 1)], egk[:]).then_inc(egb_done, 1)

            routing_turn(0)
            with dve.Fori(0, TT - 1) as g:
                routing_turn(1, g)

            dve.wait_ge(egb_done, TT)
            dve.tensor_copy(iota4[:], iota[:].unsqueeze(2).broadcast_to([P, NK, UT])).then_inc(iota4_done, 1)
            dve.wait_ge(iota4_done, 1)

            def key_and_gate_parts(it, g):
                def step(k, ins):
                    ins.then_inc(parts_done, 1)
                    wait(dve, parts_done, 6 * it + k, g, 6)

                wait(dve, egT_done, it + 1, g, 1)
                if it >= 1:
                    wait(dve, oh_done, UNITS * it, g, UNITS)
                dve.tensor_copy(key_t[:], egT[:, 0:2]).then_inc(parts_done, 1)
                step(2, dve.tensor_copy(gate_t[:, 0], egT[:, 2]))
                step(3, dve.tensor_tensor(gleft[:], egT[:, 2], gate_t[:, 0], ALU.subtract))
                step(4, dve.tensor_copy(gate_t[:, 1], gleft[:]))
                step(5, dve.tensor_tensor(gleft[:], gleft[:], gate_t[:, 1], ALU.subtract))
                step(6, dve.tensor_copy(gate_t[:, 2], gleft[:]))

            def one_hot_rows(u, it, g):
                k = UNITS * it + u
                tok = slice(UT * u, UT * (u + 1))
                shape = [P, NK, UT]
                if k >= 2:
                    wait(dve, oh_done, k - 1, g, UNITS)
                dve.tensor_tensor(eq1[:, k % 2], iota4[:], key_t[:, 0, tok].unsqueeze(1).broadcast_to(shape),
                                  ALU.is_equal).then_inc(eq1_done, 1)
                if k >= URING:
                    wait(dve, g_mm, k - URING + 1, g, UNITS)
                dve.tensor_tensor(oh2[:, u % URING], iota4[:], key_t[:, 1, tok].unsqueeze(1).broadcast_to(shape),
                                  ALU.is_equal)
                wait(dve, eq1_done, k + 1, g, UNITS)
                dve.tensor_tensor(oh1[:, u % URING], eq1[:, k % 2].unsqueeze(1).broadcast_to([P, 3, NK, UT]),
                                  gate_t[:, :, tok].unsqueeze(2).broadcast_to([P, 3, NK, UT]),
                                  ALU.mult).then_inc(oh_done, 1)

            def gate_turn(it, g=None):
                for j in range(STEP):
                    split_lo(dve, EU + (TT + it) * STEP + j + LEAD, g)
                    if j == 3:
                        key_and_gate_parts(it, g)
                    for u in units(j + 1):
                        one_hot_rows(u, it, g)

            gate_turn(0)
            with dve.Fori(0, TT - 1) as g:
                gate_turn(1, g)

            def coef(m):
                b, e = (m // GT) % 2, m % GT
                return (hq[:, b, e].rearrange("p (c t) -> p c t", c=S // CHUNK),
                        gq[:, b, :, e * CHUNK:(e + 1) * CHUNK])

            def coef_make(m, g=None):
                if m >= NK:
                    return
                if m % GT == 0:
                    b, turns = (m // GT) % 2, STEP // GT // 2
                    wait(dve, hq_in[b], 16 * (m // GT // 2 + 1), g, 16 * turns)
                    wait(dve, gq_in[b], 16 * (m // GT // 2 + 1), g, 16 * turns)
                if m >= 2:
                    wait(dve, clo_done, m - 1, g)
                a, w = coef(m)
                dve.tensor_tensor(cf[:, m % 2].rearrange("p (c t) -> p c t", c=S // CHUNK), a, w,
                                  ALU.mult).then_inc(cf_done, 1)

            def coef_lo(m, g=None):
                if m >= NK:
                    return
                wait(dve, chi_done, m + 1, g)
                dve.tensor_tensor(clo[:, m % 4], cf[:, m % 2], chi[:, m % 4], ALU.subtract).then_inc(clo_done, 1)

            def expert_v_turn(it, g=None):
                for j in range(STEP):
                    if g is not None or not deferred(EV + it * STEP + j + LEAD):
                        split_lo(dve, EV + it * STEP + j + LEAD, g)
                    coef_make(it * STEP + j + CLEAD, g)
                    coef_lo(it * STEP + j + CLEAD, g)

            for b in range(2):
                dve.wait_ge(g_stored[b], 16 * S // CHUNK // 2)
            for m in range(CLEAD):
                coef_make(m)
                coef_lo(m)
            expert_v_turn(0)
            with dve.Fori(0, NK // STEP - 2) as g:
                expert_v_turn(1, g)
            expert_v_turn(NK // STEP - 1)

            norm_dve(dve, "h2", GA - 1, h2_done)
            for s in (GA + 1, GA + 2):
                split_lo(dve, s)
            for s in range(GA, END):
                split_lo(dve, s + LEAD)
            for n in range(2 * TT):
                t, half = n // 2, n % 2
                part = slice(half * S, (half + 1) * S)
                dve.wait_ge(sg_done, n + 1)
                dve.tensor_tensor(sg[:, n % 2], sg[:, n % 2], pp[:, t, part], ALU.mult).then_inc(sgp_pre, 1)
                dve.wait_ge(sgp_pre, n + 1)
                if n >= 4:
                    dve.wait_ge(out_done[n % 4], 16 * (n // 4))
                dve.tensor_tensor(ov[:, n % 4], sg[:, n % 2], xs[:, t, part], ALU.add).then_inc(ov_done, 1)

        @block.tensor
        def _(pe):
            v_last(pe, GLU, lambda s: (p_hi[:, s - PROJ], p_lo[:, s - PROJ]),
                   lambda s: pe.wait_ge(p_lo_done, s - PROJ + 1), first=True)
            for pair in range(TT // 2):
                pe.wait_ge(pp_act, 2 * pair + 2)
                pe.wait_ge(pp_dve, 2 * pair + 2)
                norm_pe(pe, "x", pair)

            def qk_squares(n):
                pe.wait_ge(sqk_done, n + 1)
                pe.matmul(ps[0:2 * H, 2], blk[:, n], sq[:, n % 2], start=(n == 0),
                          stop=(n == 2 * CC - 1)).then_inc(qk_sum, 1)

            def qk_spread(n):
                pe.wait_ge(r3_done, 6)
                if n == 0:
                    pe.wait_ge(rt_done, 1)
                if n >= 4:
                    pe.wait_ge(qk_done, n - 3)
                pe.matmul(ps[:, QK_BANKS[n % 4]], selq[:, n], r3[:], start=True, stop=True).then_inc(qk_rms, 1)

            def v_transpose(n):
                pe.wait_ge(vT_done, n + 1)
                if n >= 2:
                    pe.wait_ge(vt_done, n - 1)
                for t in range(TT):
                    last = pe.transpose(ps[:, 4 + n % 2, t * P:(t + 1) * P], vT[:, n % 2, t * P:(t + 1) * P], ident[:])
                last.then_inc(v_tr, 1)

            def bank_wait(s):
                p = s - 2
                if p < GLU:
                    return
                if p < FG:
                    c = (p - GLU) // 2
                    pe.wait_ge(glu_done if (p - GLU) % 2 else sig_done, c + 1)
                elif p == FG:
                    pe.wait_ge(f_act, 1)
                elif p < VV:
                    pe.wait_ge(qkraw_done, p - QK + 1)
                else:
                    pe.wait_ge(vT_done, p - VV + 1)

            for s in range(GLU, WO):
                bank_wait(s)
                u_tile(pe, s, s % 2, after="x" if s == GLU else None)
                if QK < s <= VV:
                    qk_squares(s - QK - 1)
                if s == VV + 2:
                    for n in range(4):
                        qk_spread(n)
                if s > VV:
                    v_transpose(s - VV - 1)
            for n in range(4, 2 * CC):
                qk_spread(n)
            v_transpose(CC - 1)

            def att_logits(i):
                q, h = HEADS[i]
                n, rows_h = (q + 1) * P, slice((h % 2) * DH, (h % 2 + 1) * DH)
                bank = ps[:, 2 + i % 2]
                if i >= 2:
                    pe.wait_ge(exp_done, i - 1)
                pe.matmul(bank[:, :n], qk[rows_h, 2 * (h // 2), q * P:(q + 1) * P], qk[rows_h, 2 * (h // 2) + 1, :n],
                          start=True, stop=False)
                pe.matmul(bank[:, :n], self_[:, h], f3[:, :n], start=False, stop=False)
                pe.matmul(bank[:, n - P:n], identb[:], negmask[:], start=False, stop=True).then_inc(logits, 1)

            def att_transpose(i):
                q, h = HEADS[i]
                pe.wait_ge(exp_done, i + 1)
                if i >= 2:
                    pe.wait_ge(pT_done, i - 1)
                for k in range(q + 1):
                    last = pe.transpose(ps[:, 4 + i % 2, k * P:(k + 1) * P], pr[:, i % 3, k * P:(k + 1) * P], ident[:])
                last.then_inc(pT_tr, 1)

            def att_values(i):
                q, h = HEADS[i]
                pe.wait_ge(pT_done, i + 1)
                if q >= 1 and h % 4 == 0:
                    pe.wait_ge(att_done, 2 * q - 1 + h // 4)
                for k in range(q + 1):
                    last = pe.matmul(ps[:, 6 + h // 4, h % 4 * DH:(h % 4 + 2) * DH],
                                     pT_sb[:, i % 2, k * P:(k + 1) * P], vt[:, k, h * DH:(h + 2) * DH],
                                     start=(k == 0), stop=(k == q))
                last.then_inc(o_done, 1)

            pe.wait_ge(qk_done, 2 * CC)
            pe.wait_ge(f3_done, 6)
            pe.wait_ge(vt_done, CC)
            for i in range(len(HEADS) + 2):
                if i < len(HEADS):
                    att_logits(i)
                if 1 <= i <= len(HEADS):
                    att_transpose(i - 1)
                if i >= 2:
                    att_values(i - 2)
                if LN_AT <= i < LN_AT + TT:
                    t = i - LN_AT
                    pe.wait_ge(conv_done, CC * CW)
                    if t >= 2:
                        pe.wait_ge(ln_sub, t - 1)
                    for c in range(CC):
                        last = pe.transpose(ps[:, t % 2, c * P:(c + 1) * P], cy[:, c, t * P:(t + 1) * P], ident[:])
                    last.then_inc(cy_tr, 1)
            pe.wait_ge(att_done, 2 * TT)
            for pair in range(TT // 2):
                norm_pe(pe, "y", pair)
            for s in range(WO, PQ - LAST):
                v_tile(pe, s, ahi[:, s - WO], alo[:, s - WO], s == WO, after="y" if s == WO else None)
            v_last(pe, PQ, lambda s: (ahi[:, s - WO], alo[:, s - WO]), then_norm="h1")
            norm_pe(pe, "h1", 1)

            pe.wait_ge(key_in, 16)
            for s in range(PQ, EU + 1):
                n = s - PQ
                if s < EU:
                    if n >= 2:
                        pe.wait_ge(u_free, n - 1)
                    u_tile(pe, s, s % 2, after="h1" if n == 0 else None)
                if n >= 1:
                    m = n - 1
                    pe.wait_ge(u_free, m + 1)
                    if m >= 2:
                        pe.wait_ge(sc_done, m - 1)
                    for t in range(TT):
                        last = pe.matmul(ps[:, 2 + m % 2, t * NK:(t + 1) * NK], qp[:, m % 2, t * P:(t + 1) * P],
                                         kT[:, m % 2], start=True, stop=True)
                    last.then_inc(sc_mm, 1)

            def expert_u(n, g=None):
                wait(pe, u_free, 2 * PH + n - 1, g)
                u_tile(pe, EU + n, (EU + n) % 2, g)

            with pe.Fori(0, TT) as g:
                for j in range(STEP):
                    expert_u(j, g)

            def gate_turn(it, g=None):
                for j in range(STEP):
                    expert_u((TT + it) * STEP + j, g)
                    if j == 1:
                        wait(pe, egs_done, it + 1, g, 1)
                        if it >= 1:
                            wait(pe, egT_done, it, g, 1)
                        for i in range(3):
                            last = pe.transpose(ps[:, 6, i * P:(i + 1) * P], egs[:, i], ident[:])
                        last.then_inc(eg_tr, 1)
                    for u in units(j):
                        k = UNITS * it + u
                        wait(pe, oh_done, k + 1, g, UNITS)
                        if k >= 4:
                            wait(pe, g_out, k - 3, g, UNITS)
                        for t in range(UT):
                            for part in range(3):
                                last = pe.matmul(ps[:, 2 + u % 4, t * NK:(t + 1) * NK], oh2[:, u % URING, :, t],
                                                 oh1[:, u % URING, part, :, t], start=(part == 0), stop=(part == 2))
                        last.then_inc(g_mm, 1)

            gate_turn(0)
            with pe.Fori(0, TT - 1) as g:
                gate_turn(1, g)

            pe.wait_ge(g_out, UNITS * TT)

            def expert_v_turn(it, g=None, tiles=STEP):
                for j in range(tiles):
                    m = it * STEP + j
                    wait(pe, clo_done, m + 1, g)
                    v_tile(pe, EV + m, chi[:, m % 4], clo[:, m % 4], m == 0, g)

            expert_v_turn(0)
            with pe.Fori(0, NK // STEP - 2) as g:
                expert_v_turn(1, g)
            expert_v_turn(NK // STEP - 1, tiles=STEP - LAST)
            v_last(pe, GA, lambda s: (chi[:, (s - EV) % 4], clo[:, (s - EV) % 4]),
                   lambda s: pe.wait_ge(clo_done, s - EV + 1), then_norm="h2")
            norm_pe(pe, "h2", 1)
            for s in range(GA, END - LAST):
                v_tile(pe, s, ahi[:, s - GA], alo[:, s - GA], s == GA, after="h2" if s == GA else None)
            v_last(pe, END, lambda s: (ahi[:, s - GA], alo[:, s - GA]))


def kernel(**inputs):
    import numpy as np
    import concourse.bacc as bacc
    from concourse.bass_utils import run_bass_kernel_spmd as run

    a = {k: np.asarray(v) for k, v in inputs.items()}
    depth, batch = a["ln_mix"].shape[0], a["x"].shape[0]
    assert depth == 1 and batch == 1 and a["x"].shape[1:] == (S, D)

    def k_major(w):
        return w.reshape(KC, P, P).transpose(1, 0, 2).reshape(P, D)

    w_in = a["w_in"][0]
    at = 3 * DA + H
    col = lambda c0: k_major(w_in[:, c0:c0 + P])
    stream = np.zeros((END, P, D), np.float32)
    stream[PROJ:GLU] = a["w_pl_proj"][0].reshape(-1, P, D)
    for c in range(CC):
        stream[GLU + 2 * c] = col(at + DA + c * P)
        stream[GLU + 2 * c + 1] = col(at + c * P)
        stream[QK + 2 * c] = col(c * P)
        stream[QK + 2 * c + 1] = col(DA + c * P)
        stream[VV + c] = col(2 * DA + c * P)
    stream[FG].reshape(P, KC, P)[:, :, :H] = w_in[:, 3 * DA:at].reshape(KC, P, H).transpose(1, 0, 2)
    stream[WO:PQ] = a["w_out"][0].reshape(KC, P, D)
    for m in range(2 * PH):
        stream[PQ + m] = k_major(a["w_peer_q"][0][:, m * P:(m + 1) * P])
    stream[EU:EV] = a["expert_u"][0].reshape(NK, NK, KC, P).transpose(0, 3, 2, 1).reshape(NK, P, D)
    stream[EV:GA] = a["expert_v"][0].reshape(NK, NK, D)
    stream[GA:END] = a["w_pl_gate"][0].reshape(KC, P, D)

    cols = np.zeros((P, C_END), np.float32)
    for c0, n in ((C_LNMIX, "ln_mix"), (C_LNFFN, "ln_ffn"), (C_LNPL, "ln_pl")):
        cols[:, c0:c0 + KC] = a[n][0].reshape(KC, P).T
    cols[:, C_YG:C_YG + CC] = a["attn_out_norm"][0].reshape(CC, P).T
    cols[:, C_YG + CC:C_YG + KC] = a["conv_out_norm"][0].reshape(CC, P).T
    cols[:, C_QN] = np.concatenate([a["q_norm"][0]] * 2)
    cols[:, C_KN] = np.concatenate([a["k_norm"][0]] * 2)
    cols[:H, C_BF] = a["b_fgate"][0]
    cols[:, C_CB:C_CB + CC] = a["conv_b"][0].reshape(CC, P).T
    cols[:, C_CW:] = a["conv_w"][0][:, 0].reshape(CW, CC, P).transpose(2, 1, 0).reshape(P, CC * CW)
    rows = np.stack([a["conv_ln_g"][0], a["conv_ln_b"][0]])
    arrays = {
        "x_in": a["x"][0],
        "p_in": a["p"][0, 0].T.reshape(PLE // P, P, S).transpose(1, 0, 2),
        "stream_in": stream,
        "cols_in": cols,
        "rows_in": np.broadcast_to(rows, (P, 2, DA)),
        "keys_in": np.stack([a["sub_keys1"][0].T, a["sub_keys2"][0].T], 1),
    }
    arrays = {k: np.ascontiguousarray(v) for k, v in arrays.items()}
    nc = bacc.Bacc("TRN2", target_bir_lowering=False, num_devices=1)
    aps = [nc.dram_tensor(k, v.shape, F32, kind="ExternalInput").ap() for k, v in arrays.items()]
    out = nc.dram_tensor("layer_out", (S, D), F32, kind="ExternalOutput").ap()
    act_dram = nc.dram_tensor("act_dram", (NK, P, S), F32, kind="Internal").ap()
    gate_dram = nc.dram_tensor("gate_dram", (S // CHUNK, P, NK * CHUNK), F32, kind="Internal").ap()
    hybrid_layer(nc, *aps, out, act_dram, gate_dram)
    r = run(nc, [arrays], core_ids=[0])
    return np.asarray(r.results[0]["layer_out"]).reshape(1, S, D)
```
